# Optimizing a Trainium2 kernel written in Bass

```python
import math
import jax, jax.numpy as jnp
from jax import lax
import numpy as np

'''Interleaved hybrid streaming-encoder trunk (chunk-causal, CHUNK = 64 frames).

Layer i uses token mixer (i mod 2): 0 -> S5 diagonal complex state-space layer,
1 -> RetNet multi-scale retention in its chunkwise-recurrent form. Every layer is
followed by a dense SwiGLU FFN. Pre-RMSNorm before every sub-layer, plain residual
adds, one final RMSNorm.

Inputs : x (BATCH, SEQ, D_MODEL) float32 plus per-layer parameters (stacked over
         the layers that use them).
Output : (BATCH, SEQ, D_MODEL).
'''

D_MODEL = 1024
BATCH = 1
SEQ = 512
DEPTH = 2

CHUNK = 64
N_MIXERS = 2
N_S5_LAYERS = (DEPTH + 1) // 2
N_RET_LAYERS = DEPTH // 2

S5_GROUP = 16
S5_GROUPS = D_MODEL // S5_GROUP
S5_STATE = 64
S5_DT_MIN = 1e-3
S5_DT_MAX = 1e-1

RET_QK_DIM = 256
RET_HEADS = D_MODEL // RET_QK_DIM
RET_V_DIM = 2 * RET_QK_DIM
RET_QK_WIDTH = RET_HEADS * RET_QK_DIM
RET_V_WIDTH = RET_HEADS * RET_V_DIM
RET_PROJ_WIDTH = 2 * RET_QK_WIDTH + 2 * RET_V_WIDTH
ROPE_BASE = 10000.0

FFN_HIDDEN = -(-8 * D_MODEL // (3 * 256)) * 256
NORM_EPS = 1e-6

kernel_name = 'chunk_causal_s5_retention_hybrid'

def rmsnorm(x, g):
    xf = x.astype(jnp.float32)
    y = xf * lax.rsqrt(jnp.mean(jnp.square(xf), axis=-1, keepdims=True) + NORM_EPS)
    return (y * g.astype(jnp.float32)).astype(x.dtype)

def swiglu(u, w_gate, w_up, w_down):
    h = jax.nn.silu(u @ w_gate.astype(u.dtype)) * (u @ w_up.astype(u.dtype))
    return h @ w_down.astype(u.dtype)

def _linear_recurrence_combine(e1, e2):
    a1, b1 = e1
    a2, b2 = e2
    return a1 * a2, a2 * b1 + b2

def s5_mixer(u, lam_re, lam_im, log_step, b_re, b_im, c_re, c_im, d, glu_w, glu_b):
    f32 = jnp.float32
    bsz, seq, _ = u.shape
    uf = u.astype(f32).reshape(bsz, seq, S5_GROUPS, S5_GROUP)
    lam = lax.complex(lam_re.astype(f32), lam_im.astype(f32))
    step = jnp.exp(log_step.astype(f32))[:, None]
    lam_bar = jnp.exp(lam * step)
    b = lax.complex(b_re.astype(f32), b_im.astype(f32))
    b_bar = ((lam_bar - 1.0) / lam)[..., None] * b
    bu = jnp.einsum('blgn,gpn->blgp', uf.astype(jnp.complex64), b_bar)
    a = jnp.broadcast_to(lam_bar, (1, seq, S5_GROUPS, S5_STATE))
    _, states = lax.associative_scan(_linear_recurrence_combine, (a, bu), axis=1)
    c = lax.complex(c_re.astype(f32), c_im.astype(f32))
    y = jnp.einsum('gnp,blgp->blgn', c, states).real + d.astype(f32) * uf
    y = jax.nn.gelu(y.reshape(bsz, seq, D_MODEL))
    y = y * jax.nn.sigmoid(y @ glu_w.astype(f32) + glu_b.astype(f32))
    return y.astype(u.dtype)

def _rotary_tables(seq):
    inv_freq = 1.0 / (ROPE_BASE ** jnp.linspace(0.0, 1.0, RET_QK_DIM // 2, dtype=jnp.float32))
    ang = jnp.arange(seq, dtype=jnp.float32)[:, None] * inv_freq[None, :]
    return jnp.cos(ang)[None, :, None, :], jnp.sin(ang)[None, :, None, :]

def _apply_rotary(t, cos, sin):
    t1, t2 = jnp.split(t, 2, axis=-1)
    return jnp.concatenate([t1 * cos - t2 * sin, t1 * sin + t2 * cos], axis=-1)

def retention_mixer(u, w_qkvg, gn_w, w_o):
    f32 = jnp.float32
    bsz, seq, _ = u.shape
    n_chunks = seq // CHUNK
    proj = jnp.matmul(u, w_qkvg.astype(u.dtype)).astype(f32)
    q, k, v, g = jnp.split(proj, [RET_QK_WIDTH, 2 * RET_QK_WIDTH, 2 * RET_QK_WIDTH + RET_V_WIDTH], axis=-1)
    q = q.reshape(bsz, seq, RET_HEADS, RET_QK_DIM)
    k = k.reshape(bsz, seq, RET_HEADS, RET_QK_DIM) * (RET_QK_DIM ** -0.5)
    v = v.reshape(bsz, seq, RET_HEADS, RET_V_DIM)
    cos, sin = _rotary_tables(seq)
    q = _apply_rotary(q, cos, sin)
    k = _apply_rotary(k, cos, sin)

    log_gamma = jnp.log1p(-jnp.exp2(-5.0 - jnp.arange(RET_HEADS, dtype=f32)))
    pos = jnp.arange(CHUNK, dtype=f32)
    intra_decay = jnp.exp(log_gamma[:, None, None] * jnp.abs(pos[:, None] - pos[None, :]))
    q_decay = jnp.exp((pos[:, None] + 1.0) * log_gamma[None, :])
    k_decay = jnp.exp((CHUNK - 1.0 - pos)[:, None] * log_gamma[None, :])
    chunk_decay = jnp.exp(CHUNK * log_gamma)

    def to_chunks(t):
        return t.reshape(bsz, n_chunks, CHUNK, RET_HEADS, t.shape[-1]).swapaxes(0, 1)

    def step(state, qkv):
        qc, kc, vc = qkv
        scores = jnp.einsum('bihd,bjhd->bhij', qc, kc) * intra_decay
        o_intra = jnp.einsum('bhij,bjhe->bihe', scores, vc)
        o_cross = jnp.einsum('bihd,bhde->bihe', qc * q_decay[None, :, :, None], state)
        new_state = state * chunk_decay[None, :, None, None] + jnp.einsum(
            'bjhd,bjhe->bhde', kc * k_decay[None, :, :, None], vc)
        return new_state, o_intra + o_cross

    state0 = jnp.zeros((bsz, RET_HEADS, RET_QK_DIM, RET_V_DIM), f32)
    _, o = lax.scan(step, state0, (to_chunks(q), to_chunks(k), to_chunks(v)))
    o = o.swapaxes(0, 1).reshape(bsz, seq, RET_HEADS, RET_V_DIM)
    mean = jnp.mean(o, axis=-1, keepdims=True)
    var = jnp.mean(jnp.square(o - mean), axis=-1, keepdims=True)
    o = ((o - mean) * lax.rsqrt(var + NORM_EPS)).reshape(bsz, seq, RET_V_WIDTH) * gn_w.astype(f32)
    y = jax.nn.silu(g) * o
    return jnp.matmul(y.astype(u.dtype), w_o.astype(u.dtype))

def setup_inputs(seed: int = 0) -> dict:
    key = jax.random.key(seed)
    ks = jax.random.split(key, 24)
    f32 = jnp.float32
    nrm = lambda k, s, sc: jax.random.normal(k, s, f32) * sc
    x = jax.random.normal(ks[0], (BATCH, SEQ, D_MODEL), f32)

    s5_norm = 1.0 + nrm(ks[1], (N_S5_LAYERS, D_MODEL), 0.02)
    s5_lambda_re = -0.5 + nrm(ks[2], (N_S5_LAYERS, S5_GROUPS, S5_STATE), 0.01)
    s5_lambda_im = (math.pi * jnp.arange(S5_STATE, dtype=f32))[None, None, :] + nrm(
        ks[3], (N_S5_LAYERS, S5_GROUPS, S5_STATE), 0.01)
    s5_log_step = jax.random.uniform(ks[4], (N_S5_LAYERS, S5_GROUPS), f32,
                                     math.log(S5_DT_MIN), math.log(S5_DT_MAX))
    b_scale = (2.0 * S5_GROUP) ** -0.5
    s5_b_re = nrm(ks[5], (N_S5_LAYERS, S5_GROUPS, S5_STATE, S5_GROUP), b_scale)
    s5_b_im = nrm(ks[6], (N_S5_LAYERS, S5_GROUPS, S5_STATE, S5_GROUP), b_scale)
    c_scale = S5_STATE ** -0.5
    s5_c_re = nrm(ks[7], (N_S5_LAYERS, S5_GROUPS, S5_GROUP, S5_STATE), c_scale)
    s5_c_im = nrm(ks[8], (N_S5_LAYERS, S5_GROUPS, S5_GROUP, S5_STATE), c_scale)
    s5_d = nrm(ks[9], (N_S5_LAYERS, S5_GROUPS, S5_GROUP), 1.0)
    s5_glu_w = nrm(ks[10], (N_S5_LAYERS, D_MODEL, D_MODEL), D_MODEL ** -0.5)
    s5_glu_b = nrm(ks[11], (N_S5_LAYERS, D_MODEL), 0.01)

    ret_norm = 1.0 + nrm(ks[12], (N_RET_LAYERS, D_MODEL), 0.02)
    ret_w_qkvg = nrm(ks[13], (N_RET_LAYERS, D_MODEL, RET_PROJ_WIDTH), D_MODEL ** -0.5)
    ret_gn_w = 1.0 + nrm(ks[14], (N_RET_LAYERS, RET_V_WIDTH), 0.02)
    ret_w_o = nrm(ks[15], (N_RET_LAYERS, RET_V_WIDTH, D_MODEL), RET_V_WIDTH ** -0.5)

    ffn_norm = 1.0 + nrm(ks[16], (DEPTH, D_MODEL), 0.02)
    ffn_w_gate = nrm(ks[17], (DEPTH, D_MODEL, FFN_HIDDEN), D_MODEL ** -0.5)
    ffn_w_up = nrm(ks[18], (DEPTH, D_MODEL, FFN_HIDDEN), D_MODEL ** -0.5)
    ffn_w_down = nrm(ks[19], (DEPTH, FFN_HIDDEN, D_MODEL), FFN_HIDDEN ** -0.5)
    final_norm = 1.0 + nrm(ks[20], (D_MODEL,), 0.02)
    return {'x': x, 's5_norm': s5_norm, 's5_lambda_re': s5_lambda_re, 's5_lambda_im': s5_lambda_im,
            's5_log_step': s5_log_step, 's5_b_re': s5_b_re, 's5_b_im': s5_b_im,
            's5_c_re': s5_c_re, 's5_c_im': s5_c_im, 's5_d': s5_d,
            's5_glu_w': s5_glu_w, 's5_glu_b': s5_glu_b,
            'ret_norm': ret_norm, 'ret_w_qkvg': ret_w_qkvg, 'ret_gn_w': ret_gn_w, 'ret_w_o': ret_w_o,
            'ffn_norm': ffn_norm, 'ffn_w_gate': ffn_w_gate, 'ffn_w_up': ffn_w_up,
            'ffn_w_down': ffn_w_down, 'final_norm': final_norm}

def reference(x, s5_norm, s5_lambda_re, s5_lambda_im, s5_log_step, s5_b_re, s5_b_im,
              s5_c_re, s5_c_im, s5_d, s5_glu_w, s5_glu_b,
              ret_norm, ret_w_qkvg, ret_gn_w, ret_w_o,
              ffn_norm, ffn_w_gate, ffn_w_up, ffn_w_down, final_norm):
    for i in range(DEPTH):
        j = i // N_MIXERS
        if i % N_MIXERS == 0:
            x = x + s5_mixer(rmsnorm(x, s5_norm[j]), s5_lambda_re[j], s5_lambda_im[j],
                             s5_log_step[j], s5_b_re[j], s5_b_im[j], s5_c_re[j], s5_c_im[j],
                             s5_d[j], s5_glu_w[j], s5_glu_b[j])
        else:
            x = x + retention_mixer(rmsnorm(x, ret_norm[j]), ret_w_qkvg[j], ret_gn_w[j], ret_w_o[j])
        x = x + swiglu(rmsnorm(x, ffn_norm[i]), ffn_w_gate[i], ffn_w_up[i], ffn_w_down[i])
    return rmsnorm(x, final_norm)


_drawn_inputs = setup_inputs


def setup_inputs(seed=0):
    import zlib

    import numpy as np

    out = dict(_drawn_inputs(seed))
    spreads = {}
    factors = {'s5_norm': 4.563,
     's5_lambda_re': 64.0,
     's5_glu_b': 8.0,
     'ret_norm': 2.949,
     'ret_gn_w': 17.284,
     'final_norm': 8.734,
     'ffn_norm': 3.613}
    for name, (base, spread) in spreads.items():
        noise = np.random.default_rng([zlib.crc32(name.encode()), seed]).standard_normal(out[name].shape)
        drawn = base * np.exp(spread * noise) if base else spread * noise
        out[name] = __import__('jax').numpy.asarray(drawn.astype(out[name].dtype))
    for name, factor in factors.items():
        out[name] = (out[name] * factor).astype(out[name].dtype)
    return out
```

```python
from contextlib import ExitStack

import concourse.bass as bass
import numpy as np
from concourse import mybir

F32 = mybir.dt.float32
F32R = mybir.dt.float32r
I32 = mybir.dt.int32
ALU = mybir.AluOpType
ACT = mybir.ActivationFunctionType

P = 128
D = 1024
SEQ = 512
KT = D // P
TT = SEQ // P
EPS = 1e-6

G, N, ST = 64, 16, 64
J = G // 2
STEPS = 8
CH = SEQ // STEPS
JB = 4
NBLK = J // JB

H, HD, VD = 4, 256, 512
CHUNK = 64
FH = 2816
FT = FH // P
HT = FT // 2

UNIT = 2048
PAIRS = {"glu": 2, "ffn0": 11, "down0": 8, "ret": 12, "wo": 4, "ffn1": 11, "down1": 8}

V_GLU_B, V_RET, V_FFN0, V_FFN1, V_FINAL, V_GN = 0, 8, 16, 24, 32, 40
NVEC = 56


def starts(counts):
    out, at = {}, 0
    for name, n in counts.items():
        out[name] = at
        at += n
    return out


PAIR0 = starts(PAIRS)
LAST_PAIR = sum(PAIRS.values()) - 1

S5_FILLS = [("bt", 0), ("bt", 1), ("vec", 0), ("lam", 0), ("ct", 0), ("ct", 1)]
S5_FILLS += [("tb", 2 * k + ri) for k in range(4) for ri in range(2)]
S5_FILLS += [("u", k) for k in range(8)]
S5_FILLS += [("b", k) for k in range(4)]
for _k in range(4, NBLK):
    S5_FILLS += [("tb", 2 * _k), ("tb", 2 * _k + 1)]
    if _k > 4:
        S5_FILLS += [("b", _k - 1)]
S5_FILLS += [("b", NBLK - 1)]
S5_FILLS += [("strip", k) for k in range(16)]
S5_FILLS += [(kind, k) for kind in ("xt", "y", "yt") for k in range(8)]
S5_AT = {f: (n % 8, n // 8) for n, f in enumerate(S5_FILLS)}


def bank_starts():
    fills = {
        "s5": [sum(1 for b, _ in S5_AT.values() if b == k) for k in range(8)],
        "glu": [2, 2, 2, 2, 0, 0, 0, 0],
        "norm0": [0, 0, 0, 0, 0, 0, 0, 1],
        "ffn0": [11, 11, 11, 11, 0, 0, 0, 0],
        "down0": [0, 0, 0, 0, 4, 4, 0, 0],
        "norm1": [0, 0, 0, 0, 0, 0, 0, 1],
        "ret": [3 * H] * 8,
        "wo": [4, 4, 0, 0, 0, 0, 0, 0],
        "norm2": [0, 0, 0, 0, 0, 0, 0, 1],
        "ffn1": [11, 11, 11, 11, 0, 0, 0, 0],
        "down1": [0, 0, 0, 0, 4, 4, 0, 0],
        "norm3": [0, 0, 0, 0, 0, 0, 0, 1],
        "store": [1] * 8,
    }
    by_unit = {
        "glu": [0, 2, 0, 2, 0, 0, 0, 0],
        "ffn0": [0, 11, 0, 11, 0, 0, 0, 0],
        "down0": [0, 0, 0, 0, 4, 4, 0, 0],
        "ret": [0, H, 0, H, 0, H, 0, 2 * H],
        "wo": [4, 4, 0, 0, 0, 0, 0, 0],
        "ffn1": [0, 11, 0, 11, 0, 0, 0, 0],
        "down1": [0, 0, 0, 0, 4, 4, 0, 0],
    }
    free, full, at, signalled = {}, {}, [0] * 8, [0] * 8
    for name, n in fills.items():
        free[name], full[name] = list(at), list(signalled)
        at = [a + b for a, b in zip(at, n)]
        signalled = [a + b - c for a, b, c in zip(signalled, n, by_unit.get(name, [0] * 8))]
    return free, full


FREE0, FULL0 = bank_starts()


def repeated(ap, axis, n):
    ap = ap.unsqueeze(axis)
    shape = list(ap.shape)
    shape[axis] = n
    return ap.broadcast_to(shape)


def trunk(nc, x, s5_norm, lam_re, lam_im, log_step, b_re, b_im, c_re, c_im, s5_d, glu_w, glu_b,
          ret_norm, ret_w, ret_gn, ret_wo, ffn_norm, ffn_gate, ffn_up, ffn_down, final_norm,
          ident_in, rope_in, decay_in, out):
    with ExitStack() as ctx:
        def sb(stack, name, shape, dt=F32):
            return stack.enter_context(nc.sbuf_tensor(name, shape, dt))

        def sem(name):
            return ctx.enter_context(nc.semaphore(name))

        xT = sb(ctx, "xT", [P, KT, SEQ])
        w_raw = sb(ctx, "w_raw", [P, 2, UNIT])
        ident = sb(ctx, "ident", [P, P])
        ones = sb(ctx, "ones", [P, P])
        vecs = sb(ctx, "vecs", [P, NVEC])
        eps = sb(ctx, "eps", [P, 1])
        small = sb(ctx, "small", [P, 64])

        s5 = ExitStack()
        r_w = sb(s5, "s5_w", [P, 4096])
        r_1 = sb(s5, "s5_1", [P, 8192])
        r_tc = sb(s5, "s5_tc", [P, 2, J, STEPS + 1, N])
        r_3 = sb(s5, "s5_3", [P, 8192])
        u = sb(s5, "s5_u", [P, G, CH])
        states = sb(s5, "s5_states", [P, CH + 1, 2, J])
        pool_tmp = sb(s5, "s5_pool_tmp", [P, 2, JB, STEPS + 1, N])
        ct = sb(s5, "s5_ct", [P, 2, J, N])
        fb = sb(s5, "s5_fb", [P, 2, J, N])
        powers = sb(s5, "s5_powers", [P, 2, STEPS + 1, J])
        b_powers = sb(s5, "s5_b_powers", [P, 2, STEPS, J])
        step8 = sb(s5, "s5_step8", [P, 2, 2, J])
        lam_t = sb(s5, "s5_lam_t", [P, 4, J])
        gain_t = sb(s5, "s5_gain_t", [P, G])
        scan_tmp = sb(s5, "s5_scan_tmp", [P, 2, 2, J])
        s5.close()
        tb = r_w[:, 0:2048].rearrange("p (s r a) -> p s r a", s=2, r=2)
        prod = r_w[:, 2048:3072].rearrange("p (s a) -> p s a", s=2)
        bt = r_w[:, 3072:4096].rearrange("p (r j n) -> p r j n", r=2, j=J)
        x_tok = r_w[:, :].rearrange("p (t d) -> p t d", t=TT)
        xc = r_1[0:64, :].rearrange("p (t d) -> p t d", t=STEPS)
        xn = r_1[64:128, :].rearrange("p (g t n) -> p g t n", g=G, t=STEPS)
        toep = r_1[:, :].rearrange("p (g m) -> p g m", g=G)
        b_rows = r_3[0:J, 0:4096].rearrange("p (r a) -> p r a", r=2)
        rows = r_3[0:J, 4096:4096 + 28 * P].rearrange("p (s a) -> p s a", a=P)
        vec_rows = r_3[64:64 + NVEC, 4096:4096 + P]
        gain_rows = r_3[64:128, 4096 + P:4096 + P + N]
        gain_rep = r_3[64:128, 4096 + 2 * P:4096 + 3 * P]
        tbt = r_3[:, :].rearrange("p (j r m) -> p j r m", j=J, r=2)
        strip = r_3[0:N, :].rearrange("p (g m) -> p g m", g=G)
        y_chunk = r_3[:, 0:4096].rearrange("p (t a) -> p t a", t=STEPS)
        y_raw = r_3[:, 4096:8192].rearrange("p (k t) -> p k t", k=KT)
        c_rows = states[:, 0:32, :, :].rearrange("p c r j -> p (c r j)")[:, 0:2 * 4 * P] \
            .rearrange("p (r b m) -> p r b m", r=2, b=4)
        junk = states[0:64, 32:48, :, :].rearrange("p c r j -> p (c r j)")
        d_rows = pool_tmp[0:N, :, :, :, :].rearrange("p s j k n -> p (s j k n)")[:, 0:1024] \
            .rearrange("p (g n) -> p g n", g=G)

        w_hi0 = sb(ctx, "w_hi0", [P, UNIT], F32R)
        w_lo0 = sb(ctx, "w_lo0", [P, UNIT], F32R)
        w_hi1 = sb(ctx, "w_hi1", [P, UNIT], F32R)
        w_lo1 = sb(ctx, "w_lo1", [P, UNIT], F32R)
        w_hi, w_lo = [w_hi0, w_hi1], [w_lo0, w_lo1]
        tmp = sb(ctx, "tmp", [P, 8, SEQ])
        u_hi = sb(ctx, "u_hi", [P, KT, SEQ], F32R)
        u_lo = sb(ctx, "u_lo", [P, KT, SEQ], F32R)
        rope = sb(ctx, "rope", [P, 2, SEQ])
        stats = sb(ctx, "stats", [P, TT, 6])
        moments = sb(ctx, "moments", [P, TT, 2])
        o_std = sb(ctx, "o_std", [P, TT])
        o_rstd = sb(ctx, "o_rstd", [P, TT])
        sig = tmp[:, 0:2, :]
        act_raw = tmp[:, 2:4, :]
        sq = tmp[:, 4, :]
        sq_sum = tmp[:, 5, :]
        rs = tmp[:, 6, :]
        scores, _at = [], 0
        for jt in range(TT):
            scores.append(tmp[:, :, :].rearrange("p s a -> p (s a)")[:, 4 * SEQ + _at:4 * SEQ + _at + SEQ - P * jt])
            _at += SEQ - P * jt
        decay = tmp[:, 0, :]
        ffn = ExitStack()
        h_hi = sb(ffn, "h_hi", [P, FT, SEQ], F32R)
        h_lo = sb(ffn, "h_lo", [P, FT, SEQ], F32R)
        ffn.close()
        ret = ExitStack()
        y_hi = sb(ret, "y_hi", [P, 4 * H, SEQ], F32R)
        y_lo = sb(ret, "y_lo", [P, 4 * H, SEQ], F32R)
        qk = sb(ret, "qk", [P, 4, SEQ])
        v = sb(ret, "v", [P, TT, VD])
        gate = sb(ret, "gate", [P, 4, SEQ])
        ret.close()
        o_norm = v
        last = ExitStack()
        final = sb(last, "final", [P, KT, SEQ])
        out_sb = sb(last, "out_sb", [P, TT, D])
        last.close()

        bank = [ctx.enter_context(nc.psum_tensor(f"bank{b}", [P, 512], F32)) for b in range(8)]
        bank_full = [sem(f"bank_full{b}") for b in range(8)]
        bank_free = [sem(f"bank_free{b}") for b in range(8)]

        lam_loaded = sem("lam_loaded")
        ident_loaded = sem("ident_loaded")
        b_loaded = sem("b_loaded")
        vecs_loaded = sem("vecs_loaded")
        xc_loaded = sem("xc_loaded")
        c_loaded = sem("c_loaded")
        d_loaded = sem("d_loaded")
        x_loaded = sem("x_loaded")
        toep_loaded = sem("toep_loaded")
        rope_loaded = sem("rope_loaded")
        decay_loaded = sem("decay_loaded")
        consts_set = sem("consts_set")
        dve_step = sem("dve_step")
        pool_step = sem("pool_step")
        phase_ready = sem("phase_ready")
        sin_ready = sem("sin_ready")
        rows_ready = sem("rows_ready")
        gain_ready = sem("gain_ready")
        powers_ready = sem("powers_ready")
        ms_ready = sem("ms_ready")
        rms_ready = sem("rms_ready")
        rs_ready = sem("rs_ready")
        xn_ready = sem("xn_ready")
        tb_ready = sem("tb_ready")
        tc_ready = sem("tc_ready")
        toep_zeroed = sem("toep_zeroed")
        diag_ready = sem("diag_ready")
        state0_ready = sem("state0_ready")
        scan_step = sem("scan_step")
        y_hi_ready = sem("y_hi_ready")
        y_split = sem("y_split")

        w_loaded = [sem(f"w_loaded{s}") for s in range(2)]
        w_hi_ready = [sem(f"w_hi_ready{s}") for s in range(2)]
        w_lo_ready = [sem(f"w_lo_ready{s}") for s in range(2)]
        w_used = [sem(f"w_used{s}") for s in range(2)]

        glu_ready = sem("glu_ready")
        x_new = sem("x_new")
        sum_done = sem("sum_done")
        rs_done = sem("rs_done")
        ret_step = sem("ret_step")
        sq_ready = sem("sq_ready")
        u_raw_ready = sem("u_raw_ready")
        u_hi_ready = sem("u_hi_ready")
        u_split = sem("u_split")
        h_hi_ready = sem("h_hi_ready")
        h_split = sem("h_split")
        rope_ready = sem("rope_ready")
        var_ready = sem("var_ready")
        std_ready = sem("std_ready")
        ret_hi_ready = sem("ret_hi_ready")
        ret_split = sem("ret_split")
        final_ready = sem("final_ready")
        out_left = sem("out_left")
        out_right = sem("out_right")
        out_stored = sem("out_stored")

        block = ctx.enter_context(nc.Block())

        glu_v = glu_w[0].rearrange("(k p) n -> p k n", p=P)
        gate_v = [ffn_gate[i].rearrange("(k p) n -> p k n", p=P) for i in range(2)]
        up_v = [ffn_up[i].rearrange("(k p) n -> p k n", p=P) for i in range(2)]
        down_v = [ffn_down[i].rearrange("(k p) n -> p k n", p=P) for i in range(2)]
        ret_v = ret_w[0].rearrange("(k p) n -> p k n", p=P)
        wo_v = ret_wo[0].rearrange("(k p) n -> p k n", p=P)

        def s5_features(t, k):
            return t[:, :, :].rearrange("p (h b) (c t) -> p h b t c", h=2, t=STEPS)[
                :, :, k // 2, 4 * (k % 2):4 * (k % 2) + 4, :].rearrange("p h t c -> p t h c")

        def tile(t, k):
            return t[:, bass.ds(k, 1), :].rearrange("p o a -> p (o a)")

        @block.sync
        def _(sp):
            def load_unit(s, pair, src, tiles, cols):
                if not isinstance(pair, int) or pair > 0:
                    sp.wait_ge(w_lo_ready[s], pair)
                sp.dma_start(w_raw[:, s, 0:tiles * cols].rearrange("p (k n) -> p k n", k=tiles),
                             src).then_inc(w_loaded[s], 16)

            sp.dma_start(rows[:, 0, :].rearrange("j (h p) -> j h p", h=2),
                         lam_re[0].rearrange("(h j) p -> j h p", h=2)).then_inc(lam_loaded, 16)
            sp.dma_start(rows[:, 1, :].rearrange("j (h p) -> j h p", h=2),
                         lam_im[0].rearrange("(h j) p -> j h p", h=2)).then_inc(lam_loaded, 16)
            with nc.allow_non_contiguous_dma(reason="64 step sizes"):
                sp.dma_start(rows[:, 2, 0:2], log_step[0].rearrange("(h j) -> j h", h=2)).then_inc(lam_loaded, 16)
            sp.dma_start(ident[:, :], ident_in).then_inc(ident_loaded, 16)
            for ri, src in enumerate((b_re, b_im)):
                sp.dma_start(b_rows[:, ri, :].rearrange("j (h a) -> j h a", h=2),
                             src[0].rearrange("(h j) p n -> j h (p n)", h=2)).then_inc(b_loaded, 16)
            sp.dma_start(gain_rows, s5_norm[0].rearrange("(g n) -> g n", n=N)).then_inc(vecs_loaded, 16)
            for col, vec in ((V_GLU_B, glu_b[0]), (V_RET, ret_norm[0]), (V_FFN0, ffn_norm[0]),
                             (V_FFN1, ffn_norm[1]), (V_FINAL, final_norm), (V_GN, ret_gn[0])):
                n = vec.shape[0] // P
                sp.dma_start(vec_rows[col:col + n, :], vec.rearrange("(k p) -> k p", p=P)).then_inc(vecs_loaded, 16)
            for ri, src in enumerate((c_re, c_im)):
                for b in range(4):
                    sp.dma_start(c_rows[:, ri, b, :].rearrange("m (h p) -> m h p", h=2),
                                 src[0].rearrange("(h b j) n p -> b (j n) h p", h=2, b=4)[b]).then_inc(c_loaded, 16)
            for s in range(2):
                load_unit(s, 0, glu_v[:, :, 256 * s:256 * s + 256], KT, 256)
            sp.wait_ge(tc_ready, NBLK)
            sp.dma_start(d_rows, s5_d[0].partition_broadcast(N)).then_inc(d_loaded, 16)
            b, fill = S5_AT[("tb", 2 * NBLK - 1)]
            sp.wait_ge(bank_full[b], fill + 1)
            sp.wait_ge(tb_ready, NBLK)
            sp.dma_start(x_tok, x[0].rearrange("(t p) d -> p t d", p=P)).then_inc(x_loaded, 16)
            sp.wait_ge(toep_zeroed, 1)
            sp.wait_ge(diag_ready, 1)
            for r in range(STEPS):
                sp.dma_start(toep[N * r:N * r + N, :, N * r:P], strip[:, :, 0:P - N * r]).then_inc(toep_loaded, 16)
            for s in range(2):
                load_unit(s, 1, glu_v[:, :, 512 + 256 * s:768 + 256 * s], KT, 256)
            b, fill = S5_AT[("y", 7)]
            sp.wait_ge(bank_full[b], fill + 1)
            sp.dma_start(rope[:, :, :], rope_in.rearrange("p (s a) -> p s a", s=2)).then_inc(rope_loaded, 16)

            def ffn_units(layer):
                with sp.Fori(0, HT) as i:
                    load_unit(0, i + PAIR0[f"ffn{layer}"], gate_v[layer][:, :, bass.ds(i * 256, 256)], KT, 256)
                    load_unit(1, i + PAIR0[f"ffn{layer}"], up_v[layer][:, :, bass.ds(i * 256, 256)], KT, 256)
                with sp.Fori(0, KT) as i:
                    for s in range(2):
                        load_unit(s, i + PAIR0[f"down{layer}"],
                                  down_v[layer][:, HT * s:HT * s + HT, bass.ds(i * P, P)], HT, P)

            ffn_units(0)
            with sp.Fori(0, H) as h:
                pair = h * 3 + PAIR0["ret"]
                load_unit(0, pair, ret_v[:, :, bass.ds(h * HD, HD)], KT, HD)
                load_unit(1, pair, ret_v[:, :, bass.ds(h * HD + D, HD)], KT, HD)
                for s in range(2):
                    load_unit(s, pair + 1, ret_v[:, 4 * s:4 * s + 4, bass.ds(h * VD + 2 * D, VD)], 4, VD)
                load_unit(0, pair + 2, ret_v[:, :, bass.ds(h * VD + 4 * D, 256)], KT, 256)
                sp.dma_start(decay, decay_in[:, bass.ds(h * SEQ, SEQ)]).then_inc(decay_loaded, 16)
                load_unit(1, pair + 2, ret_v[:, :, bass.ds(h * VD + 4 * D + 256, 256)], KT, 256)
            with sp.Fori(0, KT // 2) as i:
                for s in range(2):
                    load_unit(s, i + PAIR0["wo"], wo_v[:, :, bass.ds(i * 256 + P * s, P)], 2 * KT, P)
            ffn_units(1)
            for t in range(TT):
                sp.wait_ge(out_left, t + 1)
                sp.wait_ge(out_right, t + 1)
                sp.dma_start(out[0, t * P:t * P + P, :], out_sb[:, t, :]).then_inc(out_stored, 16)
            sp.wait_ge(out_stored, 16 * TT)

        @block.tensor
        def _(pe):
            def s5_open(kind, n):
                b, fill = S5_AT[(kind, n)]
                if fill:
                    pe.wait_ge(bank_free[b], fill)
                return bank[b], bank_full[b]

            def s5_tables(k):
                pe.wait_ge(tb_ready, k + 1)
                for ri in range(2):
                    ps, full = s5_open("tb", 2 * k + ri)
                    for j in range(JB):
                        mm = pe.transpose(ps[:, P * j:P * j + P], tb[:, k % 2, ri, P * j:P * j + P], ident[:, :])
                    mm.then_inc(full, 1)

            def s5_inputs(k):
                for ri in range(2):
                    b, fill = S5_AT[("tb", 2 * k + ri)]
                    pe.wait_ge(bank_free[b], fill + 1)
                ps, full = s5_open("b", k)
                for j in range(JB):
                    for ri in range(2):
                        for half in range(2):
                            jj = JB * k + j
                            col = (2 * j + ri) * CH
                            mm = pe.matmul(ps[64 * half:64 * half + 64, col:col + CH],
                                           tbt[:, jj, ri, 64 * half:64 * half + 64], u[:, J * half + jj, :],
                                           start=True, stop=True)
                mm.then_inc(full, 1)

            pe.wait_ge(ident_loaded, 16)
            pe.wait_ge(b_loaded, 32)
            for ri in range(2):
                ps, full = s5_open("bt", ri)
                for n in range(N):
                    mm = pe.transpose(ps[:, J * n:J * n + J], b_rows[:, ri, n::N], ident[0:J, 0:J])
                mm.then_inc(full, 1)
            ps, full = s5_open("vec", 0)
            pe.wait_ge(vecs_loaded, 7 * 16)
            pe.wait_ge(gain_ready, 1)
            pe.transpose(ps[:, 0:NVEC], vec_rows, ident[64:64 + NVEC, 64:64 + NVEC])
            pe.transpose(ps[:, 64:128], gain_rep, ident[64:128, 64:128]).then_inc(full, 1)
            ps, full = s5_open("lam", 0)
            pe.wait_ge(rows_ready, 1)
            for i in range(4):
                mm = pe.transpose(ps[:, J * i:J * i + J], rows[:, 3 + i, :], ident[0:J, 0:J])
            mm.then_inc(full, 1)
            pe.wait_ge(c_loaded, 8 * 16)
            for ri in range(2):
                ps, full = s5_open("ct", ri)
                for b in range(4):
                    mm = pe.transpose(ps[:, P * b:P * b + P], c_rows[:, ri, b, :], ident[:, :])
                mm.then_inc(full, 1)
            for k in range(4):
                s5_tables(k)
            pe.wait_ge(xn_ready, STEPS)
            for k in range(8):
                ps, full = s5_open("u", k)
                for i in range(8):
                    mm = pe.transpose(ps[:, CH * i:CH * i + CH],
                                      xn[:, 8 * k + i, :, :].rearrange("p t n -> p (t n)"), ident[64:128, 64:128])
                mm.then_inc(full, 1)
            for k in range(8):
                b, fill = S5_AT[("u", k)]
                pe.wait_ge(bank_free[b], fill + 1)
            for k in range(4):
                s5_inputs(k)
            for k in range(4, NBLK):
                s5_tables(k)
                if k > 4:
                    s5_inputs(k - 1)
            s5_inputs(NBLK - 1)
            pe.wait_ge(tc_ready, NBLK)
            for k in range(16):
                ps, full = s5_open("strip", k)
                for i in range(4):
                    half, j = divmod(4 * k + i, J)
                    rows64 = slice(64 * half, 64 * half + 64)
                    for ri in range(2):
                        mm = pe.matmul(ps[0:N, P * i:P * i + P], fb[rows64, ri, j, :],
                                       r_tc[rows64, ri, j, 0:STEPS, :], start=(ri == 0), stop=(ri == 1))
                mm.then_inc(full, 1)
            pe.wait_ge(x_loaded, 16)
            for k in range(KT):
                ps, full = s5_open("xt", k)
                for t in range(TT):
                    mm = pe.transpose(ps[:, P * t:P * t + P], x_tok[:, t, P * k:P * k + P], ident[:, :])
                mm.then_inc(full, 1)
            pe.wait_ge(toep_loaded, 16 * STEPS)
            pe.wait_ge(scan_step, 3 * (CH - 1))
            for k in range(8):
                ps, full = s5_open("y", k)
                for j in range(4):
                    for half in range(2):
                        jj = 4 * k + j
                        rows64 = slice(64 * half, 64 * half + 64)
                        o = ps[rows64, P * j:P * j + P]
                        pe.matmul(o, u[:, J * half + jj, :], toep[:, J * half + jj, :], start=True, stop=False)
                        for ri in range(2):
                            mm = pe.matmul(o, states[rows64, 0:CH, ri, jj], r_tc[rows64, ri, jj, 1:STEPS + 1, :],
                                           start=False, stop=(ri == 1))
                mm.then_inc(full, 1)
            for k in range(8):
                b, fill = S5_AT[("y", k)]
                pe.wait_ge(bank_free[b], fill + 1)
            for k in range(8):
                ps, full = s5_open("yt", k)
                for t in range(4):
                    step, jb = 4 * (k % 2) + t, k // 2
                    mm = pe.transpose(ps[:, P * t:P * t + P], y_chunk[:, step, P * jb:P * jb + P], ident[:, :])
                mm.then_inc(full, 1)

            def product(o, w, w_cols, hi, lo, first, end):
                pe.matmul(o, w_hi[w][:, w_cols], hi, start=first, stop=False)
                pe.matmul(o, w_hi[w][:, w_cols], lo, start=False, stop=False)
                return pe.matmul(o, w_lo[w][:, w_cols], hi, start=False, stop=end)

            def open_bank(b, fill):
                pe.wait_ge(bank_free[b], fill)

            def two_tiles(s, pair, banks, fills, split, split0):
                pe.wait_ge(w_lo_ready[s], pair + 1)
                for b, fill in zip(banks, fills):
                    open_bank(b, fill)
                for k in range(KT):
                    if split is not None:
                        pe.wait_ge(split, split0 + k + 1)
                    for m, b in enumerate(banks):
                        cols = slice(256 * k + P * m, 256 * k + P * m + P)
                        mm = product(bank[b][:, :], s, cols, u_hi[:, k, :], u_lo[:, k, :], k == 0, k == KT - 1)
                        if k == KT - 1 and m == 0:
                            mm.then_inc(bank_full[b], 1)
                mm.then_inc(w_used[s], 1)

            def rms_sum(norm):
                b0 = FREE0[f"norm{norm}"][7]
                pe.wait_ge(sum_done, (KT + 1) * (norm + 1))
                open_bank(7, b0)
                pe.matmul(bank[7][:, :], ones[:, :], sq_sum, start=True, stop=True).then_inc(bank_full[7], 1)

            pe.wait_ge(y_split, 8)
            with pe.Fori(0, 2) as i:
                for s in range(2):
                    banks = [2 * s, 2 * s + 1]
                    two_tiles(s, i + PAIR0["glu"], banks, [i + FREE0["glu"][b] for b in banks], None, 0)
            rms_sum(0)

            def ffn_products(layer, norm_split0, norm):
                with pe.Fori(0, HT) as i:
                    for s in range(2):
                        banks = [2 * s, 2 * s + 1]
                        two_tiles(s, i + PAIR0[f"ffn{layer}"], banks, [i + FREE0[f"ffn{layer}"][b] for b in banks],
                                  u_split if s == 0 else None, norm_split0)
                with pe.Fori(0, KT // 2) as i:
                    for m in range(2):
                        b = 4 + m
                        open_bank(b, i + FREE0[f"down{layer}"][b])
                        for s in range(2):
                            pe.wait_ge(w_lo_ready[s], i * 2 + PAIR0[f"down{layer}"] + m + 1)
                            for k in range(HT):
                                kk = HT * s + k
                                pe.wait_ge(h_split, FT * layer + kk + 1)
                                mm = product(bank[b][:, :], s, slice(P * k, P * k + P), h_hi[:, kk, :],
                                             h_lo[:, kk, :], kk == 0, kk == FT - 1)
                            mm.then_inc(w_used[s], 1)
                rms_sum(norm)

            ffn_products(0, 0, 1)

            with pe.Fori(0, H) as h:
                pair = h * 3 + PAIR0["ret"]
                fill = [h * 3 + FREE0["ret"][b] for b in range(8)]
                two_tiles(0, pair, [0, 1], fill[0:2], u_split, 8)
                two_tiles(1, pair, [2, 3], fill[2:4], None, 0)
                for s in range(2):
                    pe.wait_ge(w_lo_ready[s], pair + 2)
                    for t in range(TT):
                        if s == 0:
                            open_bank(4 + t, fill[4 + t])
                        for k in range(4):
                            kk = 4 * s + k
                            cols = slice(VD * k, VD * k + VD)
                            a_hi, a_lo = u_hi[:, kk, P * t:P * t + P], u_lo[:, kk, P * t:P * t + P]
                            o = bank[4 + t][:, :]
                            pe.matmul(o, a_hi, w_hi[s][:, cols], start=(kk == 0), stop=False)
                            pe.matmul(o, a_hi, w_lo[s][:, cols], start=False, stop=False)
                            mm = pe.matmul(o, a_lo, w_hi[s][:, cols], start=False, stop=(kk == KT - 1))
                        if s == 1 and t < TT - 1:
                            mm.then_inc(bank_full[4 + t], 1)
                    mm.then_inc(w_used[s], 1)
                pe.wait_ge(rope_ready, h * 2 + 2)
                for jt in range(TT):
                    open_bank(jt, fill[jt] + 1)
                    for d in range(2):
                        mm = pe.matmul(bank[jt][:, 0:SEQ - P * jt], qk[:, 2 + d, P * jt:P * jt + P],
                                       qk[:, d, P * jt:SEQ], start=(d == 0), stop=(d == 1))
                    mm.then_inc(bank_full[jt], 1)
                two_tiles(0, pair + 2, [4, 5], [f + 1 for f in fill[4:6]], None, 0)
                for t in range(TT):
                    open_bank(4 + t, fill[4 + t] + 1)
                for t in range(TT):
                    open_bank(t, fill[t] + 2)
                for it in range(TT):
                    for jt in range(it + 1):
                        mm = pe.matmul(bank[it][:, :], scores[jt][:, P * (it - jt):P * (it - jt) + P], v[:, jt, :],
                                       start=(jt == 0), stop=(jt == it))
                    mm.then_inc(bank_full[it], 1)
                two_tiles(1, pair + 2, [6, 7], [f + 1 for f in fill[6:8]], None, 0)
                for m in range(4):
                    open_bank(4 + m, fill[4 + m] + 2)
                    for it in range(TT):
                        if m == 0:
                            open_bank(it, fill[it] + 3)
                        mm = pe.transpose(bank[4 + m][:, P * it:P * it + P], o_norm[:, it, P * m:P * m + P], ident[:, :])
                    mm.then_inc(bank_full[4 + m], 1)
            with pe.Fori(0, KT // 2) as i:
                for s in range(2):
                    pe.wait_ge(w_lo_ready[s], i + PAIR0["wo"] + 1)
                    open_bank(s, i + FREE0["wo"][s])
                    for k in range(4 * H):
                        pe.wait_ge(ret_split, k + 1)
                        mm = product(bank[s][:, :], s, slice(P * k, P * k + P), y_hi[:, k, :], y_lo[:, k, :],
                                     k == 0, k == 4 * H - 1)
                    mm.then_inc(w_used[s], 1)
            rms_sum(2)
            ffn_products(1, 16, 3)
            for t in range(TT):
                for half in range(2):
                    b = 2 * t + half
                    open_bank(b, FREE0["store"][b])
                    for k in range(4):
                        kk = 4 * half + k
                        pe.wait_ge(final_ready, kk + 1)
                        mm = pe.transpose(bank[b][:, P * k:P * k + P], final[:, kk, P * t:P * t + P], ident[:, :])
                    mm.then_inc(bank_full[b], 1)

        @block.scalar
        def _(act):
            def s5_full(kind, n):
                b, fill = S5_AT[(kind, n)]
                act.wait_ge(bank_full[b], fill + 1)
                return bank[b], bank_free[b]

            def copy(o, i, scale=1.0):
                return act.activation(o, i, ACT.Copy, scale=scale)

            def split_weights(s, pair):
                act.wait_ge(w_loaded[s], (pair + 1) * 16)
                if not isinstance(pair, int) or pair > 0:
                    act.wait_ge(w_used[s], pair)
                copy(w_hi[s][:, :], w_raw[:, s, :]).then_inc(w_hi_ready[s], 1)

            act.dma_start(xc, x[0].rearrange("(c t) d -> c t d", t=STEPS)).then_inc(xc_loaded, 16)
            for ri in range(2):
                ps, free = s5_full("bt", ri)
                copy(bt[:, ri, :, :].rearrange("p j n -> p n j"),
                     ps[:, :].rearrange("p (n j) -> p n j", n=N)).then_inc(free, 1)
            act.wait_ge(phase_ready, 1)
            act.activation(rows[:, 11, :], rows[:, 10, :], ACT.Sin).then_inc(sin_ready, 1)
            act.activation(rows[:, 12, :], rows[:, 10, :], ACT.Sin, scale=0.5).then_inc(sin_ready, 1)
            ps, free = s5_full("vec", 0)
            copy(vecs[:, :], ps[:, 0:NVEC])
            copy(gain_t[:, :], ps[:, 64:128]).then_inc(free, 1)
            ps, free = s5_full("lam", 0)
            copy(lam_t[:, :, :].rearrange("p i j -> p (i j)"), ps[:, 0:4 * J]).then_inc(free, 1)
            for ri in range(2):
                ps, free = s5_full("ct", ri)
                copy(ct[:, ri, :, :].rearrange("p j n -> p (j n)"), ps[:, :], -1.0 if ri else 1.0).then_inc(free, 1)
            act.wait_ge(xc_loaded, 16)
            for t in range(STEPS):
                if t:
                    act.wait_ge(ms_ready, t)
                act.activation(junk, xc[:, t, :], ACT.Square, accum_out=small[0:64, t:t + 1]).then_inc(ms_ready, 1)
            act.wait_ge(ms_ready, STEPS)
            act.wait_ge(consts_set, 1)
            act.activation(small[0:64, 8:16], small[0:64, 0:8], ACT.Sqrt, bias=eps[0:64, :],
                           scale=1.0 / D).then_inc(rms_ready, 1)
            act.wait_ge(rs_ready, 1)
            for t in range(STEPS):
                act.activation(xn[:, :, t, :], xc[:, t, :].rearrange("p (g n) -> p g n", g=G), ACT.Copy,
                               scale=small[0:64, 16 + t:17 + t]).then_inc(xn_ready, 1)

            def s5_table_out(k):
                for ri in range(2):
                    ps, free = s5_full("tb", 2 * k + ri)
                    copy(tbt[:, JB * k:JB * k + JB, ri, :], ps[:, :].rearrange("p (j m) -> p j m", j=JB)).then_inc(free, 1)

            def s5_input_out(k):
                ps, free = s5_full("b", k)
                copy(states[:, 1:CH + 1, :, JB * k:JB * k + JB].rearrange("p c r j -> p j r c"),
                     ps[:, :].rearrange("p (j r c) -> p j r c", j=JB, r=2)).then_inc(free, 1)

            for k in range(4):
                s5_table_out(k)
            for k in range(4):
                s5_input_out(k)
            for k in range(4, NBLK):
                s5_table_out(k)
                if k > 4:
                    s5_input_out(k - 1)
            s5_input_out(NBLK - 1)
            for k in range(16):
                ps, free = s5_full("strip", k)
                copy(strip[:, 4 * k:4 * k + 4, :].rearrange("p g m -> p (g m)"), ps[0:N, :]).then_inc(free, 1)
            for k in range(KT):
                ps, free = s5_full("xt", k)
                copy(xT[:, k, :], ps[:, :]).then_inc(free, 1)
            split_weights(0, 0)
            for k in range(8):
                ps, free = s5_full("y", k)
                act.activation(y_chunk[:, :, 4 * N * k:4 * N * k + 4 * N].rearrange("p t (j n) -> p j t n", j=4),
                               ps[:, :].rearrange("p (j t n) -> p j t n", j=4, t=STEPS),
                               ACT.Gelu_apprx_tanh).then_inc(free, 1)
            split_weights(1, 0)
            for k in range(8):
                b, fill = S5_AT[("yt", k)]
                act.wait_ge(bank_free[b], fill + 1)
                copy(s5_features(u_hi, k), s5_features(y_raw, k)).then_inc(y_hi_ready, 1)

            def square(t):
                act.activation(sq, tile(xT, t), ACT.Square).then_inc(sq_ready, 1)

            def norm(i):
                b = FULL0[f"norm{i}"][7]
                act.wait_ge(bank_full[7], b + 1)
                act.activation(rs, bank[7][:, :], ACT.Sqrt, bias=eps[:, :], scale=1.0 / D).then_inc(bank_free[7], 1)
                for k in range(KT if i < 3 else 0):
                    act.wait_ge(u_raw_ready, KT * i + k + 1)
                    copy(u_hi[:, k, :], act_raw[:, k % 2, :]).then_inc(u_hi_ready, 1)

            with act.Fori(0, 2) as i:
                for m in range(4):
                    if m % 2:
                        act.wait_ge(w_used[m // 2], i + PAIR0["glu"] + 1)
                    else:
                        act.wait_ge(bank_full[m], i + FULL0["glu"][m] + 1)
                    act.activation(sig[:, m % 2, :], bank[m][:, :], ACT.Sigmoid,
                                   bias=vecs[:, bass.ds(i * 4 + V_GLU_B + m, 1)]).then_inc(bank_free[m], 1)
                    if m % 2:
                        split_weights(m // 2, i + PAIR0["glu"] + 1)
                    act.wait_ge(x_new, i * 4 + m + 1)
                    square(i * 4 + m)
            norm(0)

            def ffn(layer, i_norm):
                def body(i, last_of_all):
                    for m in range(2):
                        pair = i * 2 + m + PAIR0[f"down{layer}"]
                        if not (last_of_all and m == 1):
                            split_weights(0, pair + 1)
                        act.wait_ge(bank_free[4 + m], i + FREE0[f"down{layer}"][4 + m] + 1)
                        square(i * 2 + m)
                        if not (last_of_all and m == 1):
                            split_weights(1, pair + 1)

                with act.Fori(0, HT) as i:
                    pair = i + PAIR0[f"ffn{layer}"]
                    for m in range(2):
                        if m:
                            act.wait_ge(w_used[0], pair + 1)
                        else:
                            act.wait_ge(bank_full[0], i + FULL0[f"ffn{layer}"][0] + 1)
                        act.activation(sig[:, m, :], bank[m][:, :], ACT.Silu).then_inc(bank_free[m], 1)
                    split_weights(0, pair + 1)
                    for m in range(2):
                        act.wait_ge(bank_free[2 + m], i + FREE0[f"ffn{layer}"][2 + m] + 1)
                        copy(tile(h_hi, i * 2 + m), act_raw[:, m, :]).then_inc(h_hi_ready, 1)
                    split_weights(1, pair + 1)
                if layer == 0:
                    with act.Fori(0, KT // 2) as i:
                        body(i, False)
                else:
                    with act.Fori(0, KT // 2 - 1) as i:
                        body(i, False)
                    body(KT // 2 - 1, True)
                norm(i_norm)

            ffn(0, 1)
            with act.Fori(0, H) as h:
                pair = h * 3 + PAIR0["ret"]
                free = [h * 3 + FREE0["ret"][b] for b in range(8)]
                for p in range(2):
                    for s in range(2):
                        split_weights(s, pair + p + 1)
                for t in range(TT):
                    if t < TT - 1:
                        n = 2 if t == 1 else 3
                        act.wait_ge(bank_full[4 + t], h * n + FULL0["ret"][4 + t] + 1)
                    else:
                        act.wait_ge(w_used[1], pair + 2)
                    copy(v[:, t, :], bank[4 + t][:, :]).then_inc(bank_free[4 + t], 1)
                split_weights(0, pair + 3)
                for m in range(2):
                    act.activation(gate[:, m, :], bank[4 + m][:, :], ACT.Silu).then_inc(bank_free[4 + m], 1)
                act.wait_ge(var_ready, h + 1)
                act.activation(o_std[:, :], moments[:, :, 1], ACT.Sqrt, bias=eps[:, :]).then_inc(std_ready, 1)
                split_weights(1, pair + 3)
                for m in range(2):
                    act.activation(gate[:, 2 + m, :], bank[6 + m][:, :], ACT.Silu).then_inc(bank_free[6 + m], 1)
                for m in range(4):
                    act.wait_ge(bank_free[4 + m], free[4 + m] + 3)
                    copy(tile(y_hi, h * 4 + m), act_raw[:, m % 2, :]).then_inc(ret_hi_ready, 1)
            with act.Fori(0, KT // 2) as i:
                for s in range(2):
                    act.wait_ge(bank_free[s], i + FREE0["wo"][s] + 1)
                    square(i * 2 + s)
                    split_weights(s, i + PAIR0["wo"] + 1)
            norm(2)
            ffn(1, 3)
            for t in range(TT):
                act.wait_ge(bank_full[2 * t], FULL0["store"][2 * t] + 1)
                copy(out_sb[:, t, 0:512], bank[2 * t][:, :]).then_inc(out_left, 1)

        @block.vector
        def _(dve):
            steps = [0]

            def step(ins):
                steps[0] += 1
                return ins.then_inc(dve_step, 1)

            def settle():
                dve.wait_ge(dve_step, steps[0])

            def mul(o, a, b):
                return dve.tensor_tensor(o, a, b, ALU.mult)

            def s5_full(kind, n):
                b, fill = S5_AT[(kind, n)]
                dve.wait_ge(bank_full[b], fill + 1)
                return bank[b], bank_free[b]

            def split_weights(s, pair):
                dve.wait_ge(w_hi_ready[s], pair + 1)
                dve.tensor_tensor(w_lo[s][:, :], w_raw[:, s, :], w_hi[s][:, :].bitcast(F32),
                                  ALU.subtract).then_inc(w_lo_ready[s], 1)

            step(dve.memset(eps[:, :], EPS))
            settle()
            dve.memset(ones[:, :], 1.0).then_inc(consts_set, 1)

            def exp(o, i, t0, t1, t2):
                magic = 12582912.0
                step(dve.tensor_scalar(t0, i, -87.0, 88.0, ALU.max, ALU.min))
                settle()
                step(dve.tensor_scalar(t1, t0, 1.4426950408889634, magic, ALU.mult, ALU.add))
                settle()
                step(dve.tensor_scalar(t1, t1, magic, None, ALU.subtract))
                settle()
                for c in (-0.693359375, 2.12194440e-4):
                    step(dve.scalar_tensor_tensor(out=t0, in0=t1, scalar=c, in1=t0, op0=ALU.mult, op1=ALU.add))
                    settle()
                step(dve.tensor_scalar(t2, t0, 1.0 / 5040, None, ALU.mult))
                settle()
                for n in (720, 120, 24, 6, 2, 1):
                    step(dve.scalar_tensor_tensor(out=t2, in0=t2, scalar=1.0 / n, in1=t0, op0=ALU.add, op1=ALU.mult))
                    settle()
                step(dve.tensor_scalar(o.bitcast(I32), t1, 127.0, 8388608.0, ALU.add, ALU.mult))
                settle()
                step(dve.scalar_tensor_tensor(out=o, in0=t2, scalar=1.0, in1=o, op0=ALU.add, op1=ALU.mult))
                settle()

            def row(n, w=P):
                return rows[:, n, 0:w]

            dve.wait_ge(lam_loaded, 48)
            exp(row(7, 2), row(2, 2), row(8, 2), row(9, 2), row(13, 2))
            for half in range(2):
                cols = slice(ST * half, ST * half + ST)
                for i in range(2):
                    step(dve.tensor_scalar(rows[:, 14 + i, cols], rows[:, i, cols], rows[:, 7, half:half + 1], None,
                                           ALU.mult))
            settle()
            two_pi = 2 * np.pi
            c1 = 6.28125
            c2 = float(np.float32(round((two_pi - c1) * 2**21) / 2**21))
            c3 = float(np.float32(two_pi - c1 - c2))
            step(dve.tensor_scalar(row(8), row(15), 1.0 / two_pi, 12582912.0, ALU.mult, ALU.add))
            settle()
            step(dve.tensor_scalar(row(8), row(8), 12582912.0, None, ALU.subtract))
            settle()
            a = row(15)
            for c in (c1, c2, c3):
                step(dve.scalar_tensor_tensor(out=row(9), in0=row(8), scalar=-c, in1=a, op0=ALU.mult, op1=ALU.add))
                settle()
                a = row(9)
            dve.tensor_scalar(row(10), row(9), -3.1415925, 3.1415925, ALU.max, ALU.min).then_inc(phase_ready, 1)
            exp(row(7), row(14), row(8), row(13), row(16))
            dve.wait_ge(vecs_loaded, 7 * 16)
            dve.tensor_copy(gain_rep.rearrange("g (t n) -> g t n", t=STEPS),
                            repeated(gain_rows, 1, STEPS)).then_inc(gain_ready, 1)
            dve.wait_ge(sin_ready, 2)
            step(mul(row(17), row(12), row(12)))
            settle()
            step(dve.tensor_scalar(row(17), row(17), -2.0, 1.0, ALU.mult, ALU.add))
            settle()
            step(mul(row(3), row(7), row(17)))
            step(mul(row(4), row(7), row(11)))
            step(mul(row(18), row(0), row(0)))
            step(mul(row(19), row(1), row(1)))
            settle()
            step(dve.tensor_tensor(row(18), row(18), row(19), ALU.add))
            step(dve.tensor_scalar(row(20), row(3), 1.0, None, ALU.subtract))
            settle()
            step(dve.reciprocal(row(18), row(18)))
            step(mul(row(21), row(20), row(0)))
            step(mul(row(22), row(4), row(1)))
            step(mul(row(23), row(4), row(0)))
            step(mul(row(24), row(20), row(1)))
            settle()
            step(dve.tensor_tensor(row(21), row(21), row(22), ALU.add))
            step(dve.tensor_tensor(row(23), row(23), row(24), ALU.subtract))
            settle()
            step(mul(row(5), row(21), row(18)))
            mul(row(6), row(23), row(18)).then_inc(rows_ready, 1)

            def complex_mul(o, a, b, t):
                step(mul(t[0], a, repeated(b[0], 1, 2)))
                step(mul(t[1], a, repeated(b[1], 1, 2)))
                settle()
                step(dve.tensor_tensor(o[0], t[0][:, 0], t[1][:, 1], ALU.subtract))
                step(dve.tensor_tensor(o[1], t[0][:, 1], t[1][:, 0], ALU.add))
                settle()

            step(dve.memset(powers[:, 0, 0, :], 1.0))
            step(dve.memset(powers[:, 1, 0, :], 0.0))
            b, fill = S5_AT[("lam", 0)]
            dve.wait_ge(bank_free[b], fill + 1)
            step(dve.tensor_copy(powers[:, :, 1, :], lam_t[:, 0:2, :]))
            settle()
            for have in (1, 2, 4):
                t = [prod[:, i, 0:2 * have * J].rearrange("p (r k j) -> p r k j", r=2, k=have) for i in range(2)]
                top = [repeated(powers[:, i, have, :], 1, have) for i in range(2)]
                complex_mul([powers[:, i, have + 1:2 * have + 1, :] for i in range(2)],
                            powers[:, :, 1:have + 1, :], top, t)
            t = [prod[:, i, :].rearrange("p (r k j) -> p r k j", r=2, k=STEPS) for i in range(2)]
            complex_mul([b_powers[:, i, :, :] for i in range(2)], powers[:, :, 0:STEPS, :][:, :, ::-1, :],
                        [repeated(lam_t[:, 2 + i, :], 1, STEPS) for i in range(2)], t)
            step(dve.tensor_copy(step8[:, 0, :, :], repeated(powers[:, 0, STEPS, :], 1, 2)))
            step(dve.tensor_copy(step8[:, 1, 0, :], powers[:, 1, STEPS, :]))
            dve.tensor_scalar(step8[:, 1, 1, :], powers[:, 1, STEPS, :], -1.0, None, ALU.mult).then_inc(powers_ready, 1)
            dve.wait_ge(powers_ready, 1)

            def tables(k):
                js = slice(JB * k, JB * k + JB)
                if k >= 2:
                    b, fill = S5_AT[("tb", 2 * k - 3)]
                    dve.wait_ge(bank_full[b], fill + 1)
                t = [prod[:, i, :].rearrange("p (j t n) -> p j t n", j=JB, t=STEPS) for i in range(2)]

                def two(b_first, o, op):
                    for i in range(2):
                        step(mul(t[i], repeated(bt[:, i, js, :], 2, STEPS),
                                 repeated(b_powers[:, i ^ b_first, :, js].rearrange("p t j -> p j t"), 3, N)))
                    settle()
                    return dve.tensor_tensor(o, prod[:, 0, :], prod[:, 1, :], op)

                step(two(0, tb[:, k % 2, 0, :], ALU.subtract))
                settle()
                step(two(1, tb[:, k % 2, 1, :], ALU.add))
                settle()
                dve.tensor_copy(fb[:, :, js, :], tb[:, k % 2, :, :].rearrange(
                    "p r (j t n) -> p r j t n", j=JB, t=STEPS)[:, :, :, STEPS - 1, :]).then_inc(tb_ready, 1)

            for ri in range(2):
                b, fill = S5_AT[("bt", ri)]
                dve.wait_ge(bank_free[b], fill + 1)
            tables(0)
            dve.wait_ge(rms_ready, 1)
            dve.reciprocal(small[0:64, 16:24], small[0:64, 8:16]).then_inc(rs_ready, 1)
            for k in range(1, 4):
                tables(k)
            b, fill = S5_AT[("vec", 0)]
            dve.wait_ge(bank_free[b], fill + 1)
            for k in range(8):
                ps, free = s5_full("u", k)
                mul(u[:, 8 * k:8 * k + 8, :], ps[:, :].rearrange("p (g c) -> p g c", g=8),
                    repeated(gain_t[:, 8 * k:8 * k + 8], 2, CH)).then_inc(free, 1)
            for k in range(4, NBLK):
                tables(k)

            dve.wait_ge(state0_ready, 1)
            for k in range(NBLK):
                b, fill = S5_AT[("b", k)]
                dve.wait_ge(bank_free[b], fill + 1)
            with dve.Fori(0, (CH - 1) // 9) as it:
                for k in range(9):
                    before = states[:, bass.ds(it * 9 + (k + 1), 1), :, :].rearrange("p o r j -> p (o r) j")
                    after = states[:, bass.ds(it * 9 + (k + 2), 1), :, :].rearrange("p o r j -> p (o r) j")
                    mul(scan_tmp[:, :, :, :], repeated(before, 1, 2), step8[:, :, :, :]).then_inc(scan_step, 1)
                    dve.wait_ge(scan_step, it * 27 + (3 * k + 1))
                    dve.tensor_tensor(after, after, scan_tmp[:, 0, :, :], ALU.add).then_inc(scan_step, 1)
                    dve.wait_ge(scan_step, it * 27 + (3 * k + 2))
                    dve.tensor_tensor(after, after, scan_tmp[:, 1, ::-1, :], ALU.add).then_inc(scan_step, 1)
                    dve.wait_ge(scan_step, it * 27 + (3 * k + 3))

            split_weights(0, 0)

            def y_low(k):
                dve.wait_ge(y_hi_ready, k + 1)
                dve.tensor_tensor(s5_features(u_lo, k), s5_features(y_raw, k), s5_features(u_hi, k).bitcast(F32),
                                  ALU.subtract).then_inc(y_split, 1)

            for k in range(8):
                ps, free = s5_full("yt", k)
                dve.tensor_copy(s5_features(y_raw, k),
                                ps[:, :].rearrange("p (t h c) -> p t h c", t=4, h=2)).then_inc(free, 1)
                if k:
                    y_low(k - 1)
            y_low(7)
            split_weights(1, 0)

            def clear_sum():
                dve.memset(sq_sum, 0.0).then_inc(sum_done, 1)

            def add_square(i, t):
                dve.wait_ge(sq_ready, t + (KT * i + 1))
                dve.wait_ge(sum_done, t + ((KT + 1) * i + 1))
                dve.tensor_tensor(sq_sum, sq_sum, sq, ALU.add).then_inc(sum_done, 1)

            def add_to_x(t, a):
                return dve.tensor_tensor(tile(xT, t), a, tile(xT, t), ALU.add)

            def norm(i, gain_col):
                dve.wait_ge(bank_free[7], FREE0[f"norm{i}"][7] + 1)
                dve.reciprocal(rs, rs).then_inc(rs_done, 1)
                dve.wait_ge(rs_done, i + 1)

                def low(k):
                    dve.wait_ge(u_hi_ready, KT * i + k + 1)
                    dve.tensor_tensor(u_lo[:, k, :], act_raw[:, k % 2, :], u_hi[:, k, :].bitcast(F32),
                                      ALU.subtract).then_inc(u_split, 1)

                for k in range(KT):
                    if i == 3:
                        o, ready = final[:, k, :], final_ready
                    else:
                        o, ready = act_raw[:, k % 2, :], u_raw_ready
                        if k >= 2:
                            dve.wait_ge(u_split, KT * i + k - 1)
                    dve.scalar_tensor_tensor(out=o, in0=xT[:, k, :], scalar=vecs[:, gain_col + k:gain_col + k + 1],
                                             in1=rs, op0=ALU.mult, op1=ALU.mult).then_inc(ready, 1)
                    if i < 3 and k:
                        low(k - 1)
                if i < 3:
                    low(KT - 1)

            clear_sum()
            with dve.Fori(0, 2) as i:
                for m in range(4):
                    dve.wait_ge(bank_free[m], i + FREE0["glu"][m] + 1)
                    mul(act_raw[:, m % 2, :], sig[:, m % 2, :], tile(y_raw, i * 4 + m)).then_inc(glu_ready, 1)
                    dve.wait_ge(glu_ready, i * 4 + m + 1)
                    add_to_x(i * 4 + m, act_raw[:, m % 2, :]).then_inc(x_new, 1)
                    add_square(0, i * 4 + m)
                    if m % 2:
                        split_weights(m // 2, i + PAIR0["glu"] + 1)
            norm(0, V_FFN0)

            def ffn(layer, i_norm, gain_col):
                def body(i, last_of_all):
                    for m in range(2):
                        pair = i * 2 + m + PAIR0[f"down{layer}"]
                        if not (last_of_all and m == 1):
                            split_weights(0, pair + 1)
                        dve.wait_ge(w_used[1], pair + 1)
                        add_to_x(i * 2 + m, bank[4 + m][:, :]).then_inc(bank_free[4 + m], 1)
                        add_square(i_norm, i * 2 + m)
                        if not (last_of_all and m == 1):
                            split_weights(1, pair + 1)

                with dve.Fori(0, HT) as i:
                    pair = i + PAIR0[f"ffn{layer}"]
                    split_weights(0, pair + 1)
                    for m in range(2):
                        if m:
                            dve.wait_ge(w_used[1], pair + 1)
                        else:
                            dve.wait_ge(bank_full[2], i + FULL0[f"ffn{layer}"][2] + 1)
                        dve.wait_ge(bank_free[m], i + FREE0[f"ffn{layer}"][m] + 1)
                        mul(act_raw[:, m, :], bank[2 + m][:, :], sig[:, m, :]).then_inc(bank_free[2 + m], 1)
                        dve.wait_ge(h_hi_ready, i * 2 + (FT * layer + m + 1))
                        dve.tensor_tensor(tile(h_lo, i * 2 + m), act_raw[:, m, :],
                                          tile(h_hi, i * 2 + m).bitcast(F32), ALU.subtract).then_inc(h_split, 1)
                    split_weights(1, pair + 1)
                    dve.wait_ge(h_split, i * 2 + (FT * layer + 2))
                clear_sum()
                if layer == 0:
                    with dve.Fori(0, KT // 2) as i:
                        body(i, False)
                else:
                    with dve.Fori(0, KT // 2 - 1) as i:
                        body(i, False)
                    body(KT // 2 - 1, True)
                norm(i_norm, gain_col)

            ffn(0, 1, V_RET)

            dve.wait_ge(rope_loaded, 16)
            with dve.Fori(0, H) as h:
                pair = h * 3 + PAIR0["ret"]
                free = [h * 3 + FREE0["ret"][b] for b in range(8)]
                t_bufs = [tmp[:, 1, :], tmp[:, 2, :], tmp[:, 3, :], tmp[:, 7, :]]

                def full(b, per_head, nth):
                    dve.wait_ge(bank_full[b], h * per_head + (FULL0["ret"][b] + nth))

                def rotate(which):
                    lo, hi = bank[2 * which], bank[2 * which + 1]
                    full(2 * which, 3, 1)
                    dve.wait_ge(w_used[which], pair + 1)
                    mul(t_bufs[0], lo[:, :], rope[:, 0, :])
                    mul(t_bufs[1], lo[:, :], rope[:, 1, :]).then_inc(bank_free[2 * which], 1)
                    mul(t_bufs[2], hi[:, :], rope[:, 1, :])
                    mul(t_bufs[3], hi[:, :], rope[:, 0, :]).then_inc(bank_free[2 * which + 1], 1)
                    dve.wait_ge(bank_free[2 * which + 1], free[2 * which + 1] + 1)
                    dve.tensor_tensor(qk[:, 2 * which, :], t_bufs[0], t_bufs[2], ALU.subtract)
                    dve.tensor_tensor(qk[:, 2 * which + 1, :], t_bufs[1], t_bufs[3], ALU.add).then_inc(rope_ready, 1)
                    dve.wait_ge(rope_ready, h * 2 + (which + 1))

                for which in range(2):
                    split_weights(which, pair + 1)
                    rotate(which)
                for s in range(2):
                    split_weights(s, pair + 2)
                dve.wait_ge(decay_loaded, h * 16 + 16)
                for jt in range(TT):
                    full(jt, 2 if jt % 2 else 3, 1 if jt % 2 else 2)
                    w = SEQ - P * jt
                    mul(scores[jt], bank[jt][:, 0:w], decay[:, 0:w]).then_inc(bank_free[jt], 1)
                for it in range(TT):
                    full(it, 2 if it % 2 else 3, 2 if it % 2 else 3)
                    dve.bn_stats(stats[:, it, :], bank[it][:, :]).then_inc(ret_step, 1)
                dve.wait_ge(ret_step, h * 5 + 4)
                split_weights(0, pair + 3)
                for it in range(TT):
                    last = dve.bn_aggr(moments[:, it, :], stats[:, it, :])
                last.then_inc(var_ready, 1)
                dve.wait_ge(std_ready, h + 1)
                dve.reciprocal(o_rstd[:, :], o_std[:, :]).then_inc(ret_step, 1)
                dve.wait_ge(ret_step, h * 5 + 5)
                for it in range(TT):
                    dve.tensor_scalar(o_norm[:, it, :], bank[it][:, :], moments[:, it, 0:1], o_rstd[:, it:it + 1],
                                      ALU.subtract, ALU.mult).then_inc(bank_free[it], 1)
                split_weights(1, pair + 3)

                def low(m):
                    dve.wait_ge(ret_hi_ready, h * 4 + (m + 1))
                    dve.tensor_tensor(tile(y_lo, h * 4 + m), act_raw[:, m % 2, :], tile(y_hi, h * 4 + m).bitcast(F32),
                                      ALU.subtract).then_inc(ret_split, 1)

                for m in range(4):
                    full(4 + m, [3, 2, 3, 1][m], [3, 2, 3, 1][m])
                    dve.wait_ge(bank_free[4 + m], free[4 + m] + 2)
                    if m >= 2:
                        dve.wait_ge(ret_split, h * 4 + (m - 1))
                    dve.scalar_tensor_tensor(out=act_raw[:, m % 2, :], in0=bank[4 + m][:, :],
                                             scalar=vecs[:, bass.ds(h * 4 + (V_GN + m), 1)], in1=gate[:, m, :],
                                             op0=ALU.mult, op1=ALU.mult).then_inc(bank_free[4 + m], 1)
                    if m:
                        low(m - 1)
                low(3)
                dve.wait_ge(ret_split, h * 4 + 4)
            clear_sum()
            with dve.Fori(0, KT // 2) as i:
                for s in range(2):
                    dve.wait_ge(w_used[s], i + PAIR0["wo"] + 1)
                    add_to_x(i * 2 + s, bank[s][:, :]).then_inc(bank_free[s], 1)
                    add_square(2, i * 2 + s)
                    split_weights(s, i + PAIR0["wo"] + 1)
            norm(2, V_FFN1)
            ffn(1, 3, V_FINAL)
            for t in range(TT):
                dve.wait_ge(bank_full[2 * t + 1], FULL0["store"][2 * t + 1] + 1)
                dve.tensor_copy(out_sb[:, t, 512:1024], bank[2 * t + 1][:, :]).then_inc(out_right, 1)

        @block.gpsimd
        def _(pool):
            steps = [0]

            def step(ins):
                steps[0] += 1
                ins.then_inc(pool_step, 1)

            def settle():
                pool.wait_ge(pool_step, steps[0])

            def mul(o, a, b):
                return pool.tensor_tensor(o, a, b, ALU.mult)

            for ri in range(2):
                b, fill = S5_AT[("ct", ri)]
                pool.wait_ge(bank_free[b], fill + 1)
            pool.memset(states[:, 0, :, :], 0.0).then_inc(state0_ready, 1)
            pool.wait_ge(powers_ready, 1)
            for k in range(NBLK):
                js = slice(JB * k, JB * k + JB)
                t = [pool_tmp[:, i, :, :, :] for i in range(2)]
                c = [repeated(ct[:, i, js, :], 2, STEPS + 1) for i in range(2)]
                w = [repeated(powers[:, i, :, js].rearrange("p k j -> p j k"), 3, N) for i in range(2)]
                step(mul(t[0], c[0], w[0]))
                step(mul(t[1], c[1], w[1]))
                settle()
                step(pool.tensor_tensor(r_tc[:, 0, js, :, :], t[0], t[1], ALU.add))
                settle()
                step(mul(t[0], c[1], w[0]))
                step(mul(t[1], c[0], w[1]))
                settle()
                pool.tensor_tensor(r_tc[:, 1, js, :, :], t[0], t[1], ALU.subtract).then_inc(tc_ready, 1)
                pool.wait_ge(tc_ready, k + 1)
            b, fill = S5_AT[("u", 7)]
            pool.wait_ge(bank_full[b], fill + 1)
            pool.memset(toep, 0.0).then_inc(toep_zeroed, 1)
            pool.wait_ge(d_loaded, 16)
            step(mul(d_rows, d_rows, repeated(ident[0:N, 0:N], 1, G)))
            settle()
            b, fill = S5_AT[("strip", 15)]
            pool.wait_ge(bank_free[b], fill + 1)
            pool.tensor_tensor(strip[:, :, 0:N], strip[:, :, 0:N], d_rows, ALU.add).then_inc(diag_ready, 1)


_INS = ["x", "s5_norm", "s5_lambda_re", "s5_lambda_im", "s5_log_step", "s5_b_re", "s5_b_im", "s5_c_re", "s5_c_im",
        "s5_d", "s5_glu_w", "s5_glu_b", "ret_norm", "ret_w_qkvg", "ret_gn_w", "ret_w_o", "ffn_norm", "ffn_w_gate",
        "ffn_w_up", "ffn_w_down", "final_norm"]


def _constants():
    f = np.float32
    inv_freq = (f(1.0) / (f(10000.0) ** np.linspace(0.0, 1.0, HD // 2, dtype=f))).astype(f)
    angle = (np.arange(SEQ, dtype=f)[:, None] * inv_freq[None, :]).astype(f).astype(np.float64)
    rope = np.concatenate([np.cos(angle).T, np.sin(angle).T], axis=1).astype(f)
    log_gamma = np.log1p(-np.exp2(-5.0 - np.arange(H)))
    key, query = np.arange(P)[:, None], np.arange(SEQ)[None, :]
    decay = np.exp(log_gamma[:, None, None] * np.abs(query - key)) * HD ** -0.5
    decay = np.where(query // CHUNK >= key // CHUNK, decay, 0.0)
    decay = np.ascontiguousarray(decay.transpose(1, 0, 2)).reshape(P, H * SEQ).astype(f)
    return {"const_ident": np.eye(P, dtype=f), "const_rope": rope, "const_decay": decay}


def kernel(**inputs):
    import concourse.bacc as _bacc
    from concourse.bass_utils import run_bass_kernel_spmd as _run

    nc = _bacc.Bacc("TRN2", target_bir_lowering=False, num_devices=1)
    arrays, args = {}, []
    for name in _INS:
        arrays[f"in_{name}_dram"] = np.ascontiguousarray(inputs[name])
    for name, a in _constants().items():
        arrays[f"in_{name}_dram"] = a
    for name, a in arrays.items():
        args.append(nc.dram_tensor(name, a.shape, mybir.dt.from_np(a.dtype), kind="ExternalInput").ap())
    args.append(nc.dram_tensor("out_0_dram", (1, SEQ, D), F32, kind="ExternalOutput").ap())
    trunk(nc, *args)
    r = _run(nc, [arrays], core_ids=[0])
    return r.results[0]["out_0_dram"]
```

```python
from contextlib import ExitStack

import concourse.bass as bass
import numpy as np
from concourse import mybir

F32 = mybir.dt.float32
F32R = mybir.dt.float32r
I32 = mybir.dt.int32
ALU = mybir.AluOpType
ACT = mybir.ActivationFunctionType

P = 128
D = 1024
SEQ = 512
KT = D // P
TT = SEQ // P
EPS = 1e-6

G, N, ST = 64, 16, 64
J = G // 2
STEPS = 8
CH = SEQ // STEPS
JB = 4
NBLK = J // JB

H, HD, VD = 4, 256, 512
CHUNK = 64
FH = 2816
FT = FH // P
HT = FT // 2

UNIT = 2048
PAIRS = {"glu": 2, "ffn0": 11, "down0": 8, "ret": 12, "wo": 4, "ffn1": 11, "down1": 8}

V_GLU_B, V_RET, V_FFN0, V_FFN1, V_FINAL, V_GN = 0, 8, 16, 24, 32, 40
NVEC = 56


def starts(counts):
    out, at = {}, 0
    for name, n in counts.items():
        out[name] = at
        at += n
    return out


PAIR0 = starts(PAIRS)
LAST_PAIR = sum(PAIRS.values()) - 1

S5_FILLS = [("bt", 0), ("bt", 1), ("vec", 0), ("lam", 0), ("ct", 0), ("ct", 1)]
S5_FILLS += [("tb", 0), ("tb", 1)] + [("u", k) for k in range(5)] + [("tb", 2), ("tb", 3)]
S5_FILLS += [("u", k) for k in range(5, 8)] + [("b", 0)]
for _k in range(2, NBLK):
    S5_FILLS += [("tb", 2 * _k), ("tb", 2 * _k + 1), ("b", _k - 1)]
S5_FILLS += [("b", NBLK - 1)]
S5_FILLS += [("strip", k) for k in range(6)]
S5_FILLS += [("xt", k) for k in range(8)]
S5_FILLS += [("strip", k) for k in range(6, NBLK)]
S5_FILLS += [("y", k) for k in range(8)] + [("yt", k) for k in range(8)]
S5_AT = {f: (n % 8, n // 8) for n, f in enumerate(S5_FILLS)}


def bank_starts():
    fills = {
        "s5": [sum(1 for b, _ in S5_AT.values() if b == k) for k in range(8)],
        "glu": [2, 2, 2, 2, 0, 0, 0, 0],
        "norm0": [0, 0, 0, 0, 0, 0, 0, 1],
        "ffn0": [11, 11, 11, 11, 0, 0, 0, 0],
        "down0": [0, 0, 0, 0, 4, 4, 0, 0],
        "norm1": [0, 0, 0, 0, 0, 0, 1, 1],
        "ret": [3 * H] * 8,
        "wo": [4, 4, 0, 0, 0, 0, 0, 0],
        "norm2": [0, 0, 0, 0, 0, 0, 0, 1],
        "ffn1": [11, 11, 11, 11, 0, 0, 0, 0],
        "down1": [0, 0, 0, 0, 4, 4, 0, 0],
        "norm3": [0, 0, 0, 0, 0, 0, 0, 1],
        "store": [1] * 8,
    }
    by_unit = {
        "glu": [0, 2, 0, 2, 0, 0, 0, 0],
        "ffn0": [0, 11, 0, 11, 0, 0, 0, 0],
        "down0": [0, 0, 0, 0, 4, 4, 0, 0],
        "ret": [0, H, 0, H, 0, H, 0, 2 * H],
        "wo": [4, 4, 0, 0, 0, 0, 0, 0],
        "ffn1": [0, 11, 0, 11, 0, 0, 0, 0],
        "down1": [0, 0, 0, 0, 4, 4, 0, 0],
    }
    free, full, at, signalled = {}, {}, [0] * 8, [0] * 8
    for name, n in fills.items():
        free[name], full[name] = list(at), list(signalled)
        at = [a + b for a, b in zip(at, n)]
        signalled = [a + b - c for a, b, c in zip(signalled, n, by_unit.get(name, [0] * 8))]
    return free, full


FREE0, FULL0 = bank_starts()


def repeated(ap, axis, n):
    ap = ap.unsqueeze(axis)
    shape = list(ap.shape)
    shape[axis] = n
    return ap.broadcast_to(shape)


def trunk(nc, x, s5_norm, lam_re, lam_im, log_step, b_re, b_im, c_re, c_im, s5_d, glu_w, glu_b,
          ret_norm, ret_w, ret_gn, ret_wo, ffn_norm, ffn_gate, ffn_up, ffn_down, final_norm,
          ident_in, rope_in, decay_in, out):
    with ExitStack() as ctx:
        def sb(stack, name, shape, dt=F32):
            return stack.enter_context(nc.sbuf_tensor(name, shape, dt))

        def sem(name):
            return ctx.enter_context(nc.semaphore(name))

        xT = sb(ctx, "xT", [P, KT, SEQ])
        w_raw = sb(ctx, "w_raw", [P, 2, UNIT])
        ident = sb(ctx, "ident", [P, P])
        ones = sb(ctx, "ones", [P, P])
        vecs = sb(ctx, "vecs", [P, NVEC])
        eps = sb(ctx, "eps", [P, 1])
        small = sb(ctx, "small", [P, 64])

        s5 = ExitStack()
        r_w = sb(s5, "s5_w", [P, 4096])
        r_1 = sb(s5, "s5_1", [P, 8192])
        r_tc = sb(s5, "s5_tc", [P, 2, J, STEPS, N])
        r_3 = sb(s5, "s5_3", [P, 8192])
        u = sb(s5, "s5_u", [P, G, CH])
        states = sb(s5, "s5_states", [P, CH + 1, 2, J])
        pool_tmp = sb(s5, "s5_pool_tmp", [P, 2, JB, STEPS, N])
        ct = sb(s5, "s5_ct", [P, 2, J, N])
        fb = sb(s5, "s5_fb", [P, 2, J, 2 * N])
        powers = sb(s5, "s5_powers", [P, 2, STEPS + 1, J])
        b_powers = sb(s5, "s5_b_powers", [P, 2, STEPS, J])
        step8 = sb(s5, "s5_step8", [P, 2, 2, J])
        lam_t = sb(s5, "s5_lam_t", [P, 4, J])
        scan_tmp = sb(s5, "s5_scan_tmp", [P, 2, 2, J])
        d_diag = sb(s5, "s5_d_diag", [2 * N, J, N])
        s5.close()
        over = ExitStack()
        sb(over, "below_r_3", [P, 4096 + 8192 + 8192])
        g_hi = sb(over, "g_hi", [P, KT, SEQ], F32R)
        g_lo = sb(over, "g_lo", [P, KT, SEQ], F32R)
        sb(over, "below_pool_tmp", [P, 4096 + (CH + 1) * 2 * J])
        y_chunk = sb(over, "y_chunk", [P, 2, STEPS, P])
        y_raw = sb(over, "y_raw", [P, 2, 2, SEQ])
        over.close()
        tb = r_w[:, 0:2048].rearrange("p (s r a) -> p s r a", s=2, r=2)
        prod = r_w[:, 2048:3072].rearrange("p (s a) -> p s a", s=2)
        bt = r_w[:, 3072:4096].rearrange("p (r j n) -> p r j n", r=2, j=J)
        x_tok = r_w[:, :].rearrange("p (t d) -> p t d", t=TT)
        xc = r_1[0:64, :].rearrange("p (t d) -> p t d", t=STEPS)
        xn = r_1[64:128, :].rearrange("p (g t n) -> p g t n", g=G, t=STEPS)
        toep = r_1[:, :].rearrange("p (g m) -> p g m", g=G)
        b_rows = r_3[0:J, 0:4096].rearrange("p (r a) -> p r a", r=2)
        rows = r_3[0:J, 4096:4096 + 28 * P].rearrange("p (s a) -> p s a", a=P)
        vec_rows = r_3[64:64 + NVEC, 4096:4096 + P]
        gain_wide = r_3[:, 8192 - J * N:8192]
        tbt = r_3[:, :].rearrange("p (j r m) -> p j r m", j=J, r=2)
        strip = r_3[0:2 * N, 0:4096].rearrange("p (j m) -> p j m", j=J)
        c_rows = states[:, 0:32, :, :].rearrange("p c r j -> p (c r j)")[:, 0:2 * 4 * P] \
            .rearrange("p (r b m) -> p r b m", r=2, b=4)
        junk = states[0:64, 32:48, :, :].rearrange("p c r j -> p (c r j)")
        d_gain = pool_tmp[0:2 * N, 0, :, :, :].rearrange("p j k n -> p (j k n)")
        d_mask = small[0:2 * N, 40:40 + N]

        w_hi0 = sb(ctx, "w_hi0", [P, UNIT], F32R)
        w_lo0 = sb(ctx, "w_lo0", [P, UNIT], F32R)
        w_hi1 = sb(ctx, "w_hi1", [P, UNIT], F32R)
        w_lo1 = sb(ctx, "w_lo1", [P, UNIT], F32R)
        w_hi, w_lo = [w_hi0, w_hi1], [w_lo0, w_lo1]
        tmp = sb(ctx, "tmp", [P, 8, SEQ])
        last = ExitStack()
        final = sb(last, "final", [P, KT, SEQ])
        last.close()
        u_hi = sb(ctx, "u_hi", [P, KT, SEQ], F32R)
        u_lo = sb(ctx, "u_lo", [P, KT, SEQ], F32R)
        rope = sb(ctx, "rope", [P, 2, SEQ])
        stats = sb(ctx, "stats", [P, TT, 6])
        moments = sb(ctx, "moments", [P, TT, 2])
        o_std = sb(ctx, "o_std", [P, TT])
        o_rstd = sb(ctx, "o_rstd", [P, TT])
        sig = tmp[:, 0:2, :]
        act_raw = tmp[:, 2:4, :]
        y_whole = tmp[:, 6, :]
        sq = tmp[:, 4, :]
        sq_sum = tmp[:, 5, :]
        rs = tmp[:, 7, :]
        rms_col, rs_col = small[:, 32:36], small[:, 36:40]
        scores, _at = [], 0
        for jt in range(TT):
            scores.append(tmp[:, :, :].rearrange("p s a -> p (s a)")[:, 4 * SEQ + _at:4 * SEQ + _at + SEQ - P * jt])
            _at += SEQ - P * jt
        decay = tmp[:, 0, :]
        ffn = ExitStack()
        h_hi = sb(ffn, "h_hi", [P, FT, SEQ], F32R)
        h_lo = sb(ffn, "h_lo", [P, FT, SEQ], F32R)
        ffn.close()
        ret = ExitStack()
        y_hi = sb(ret, "y_hi", [P, 4 * H, SEQ], F32R)
        y_lo = sb(ret, "y_lo", [P, 4 * H, SEQ], F32R)
        qk = sb(ret, "qk", [P, 4, SEQ])
        v = sb(ret, "v", [P, TT, VD])
        gate = sb(ret, "gate", [P, 4, SEQ])
        ret.close()
        o_norm = v
        last = ExitStack()
        out_sb = sb(last, "out_sb", [P, TT, D])
        last.close()

        bank = [ctx.enter_context(nc.psum_tensor(f"bank{b}", [P, 512], F32)) for b in range(8)]
        bank_full = [sem(f"bank_full{b}") for b in range(8)]
        bank_free = [sem(f"bank_free{b}") for b in range(8)]

        lam_loaded = sem("lam_loaded")
        ident_loaded = sem("ident_loaded")
        b_loaded = sem("b_loaded")
        vecs_loaded = sem("vecs_loaded")
        xc_loaded = sem("xc_loaded")
        c_loaded = sem("c_loaded")
        d_loaded = sem("d_loaded")
        x_loaded = sem("x_loaded")
        toep_loaded = [sem(f"toep_loaded{n}") for n in range(2)]
        rope_loaded = sem("rope_loaded")
        decay_loaded = sem("decay_loaded")
        consts_set = sem("consts_set")
        dve_step = sem("dve_step")
        pool_step = sem("pool_step")
        phase_ready = sem("phase_ready")
        sin_ready = sem("sin_ready")
        rows_ready = sem("rows_ready")
        gain_loaded = sem("gain_loaded")
        bt_ready = sem("bt_ready")
        fb_zeroed = sem("fb_zeroed")
        fb_ready = sem("fb_ready")
        powers_ready = sem("powers_ready")
        ms_ready = sem("ms_ready")
        rms_ready = sem("rms_ready")
        rs_ready = sem("rs_ready")
        xn_ready = sem("xn_ready")
        tb_ready = sem("tb_ready")
        tc_ready = sem("tc_ready")
        toep_zeroed = sem("toep_zeroed")
        diag_ready = sem("diag_ready")
        state0_ready = sem("state0_ready")
        scan_step = [sem(f"scan_step{n}") for n in range(2)]
        y_hi_ready = sem("y_hi_ready")
        y_split = sem("y_split")

        w_loaded = [sem(f"w_loaded{s}") for s in range(2)]
        w_hi_ready = [sem(f"w_hi_ready{s}") for s in range(2)]
        w_lo_ready = [sem(f"w_lo_ready{s}") for s in range(2)]
        w_used = [sem(f"w_used{s}") for s in range(2)]

        glu_ready = sem("glu_ready")
        x_new = sem("x_new")
        sum_done = sem("sum_done")
        rs_done = sem("rs_done")
        rms_col_ready = sem("rms_col_ready")
        rs_col_ready = sem("rs_col_ready")
        gate_ready = sem("gate_ready")
        ret_step = sem("ret_step")
        sq_ready = sem("sq_ready")
        u_raw_ready = sem("u_raw_ready")
        u_hi_ready = sem("u_hi_ready")
        u_split = sem("u_split")
        h_raw_ready = sem("h_raw_ready")
        h_hi_ready = sem("h_hi_ready")
        h_split = sem("h_split")
        rope_scaled = sem("rope_scaled")
        rope_ready = sem("rope_ready")
        var_ready = sem("var_ready")
        std_ready = sem("std_ready")
        ret_hi_ready = sem("ret_hi_ready")
        ret_split = sem("ret_split")
        final_ready = sem("final_ready")
        out_left = sem("out_left")
        out_right = sem("out_right")
        out_stored = sem("out_stored")

        block = ctx.enter_context(nc.Block())

        glu_v = glu_w[0].rearrange("(k p) n -> p k n", p=P)
        gate_v = [ffn_gate[i].rearrange("(k p) n -> p k n", p=P) for i in range(2)]
        up_v = [ffn_up[i].rearrange("(k p) n -> p k n", p=P) for i in range(2)]
        down_v = [ffn_down[i].rearrange("(k p) n -> p k n", p=P) for i in range(2)]
        ret_v = ret_w[0].rearrange("(k p) n -> p k n", p=P)
        wo_v = ret_wo[0].rearrange("(k p) n -> p k n", p=P)

        def tile(t, k):
            return t[:, bass.ds(k, 1), :].rearrange("p o a -> p (o a)")

        @block.sync
        def _(sp):
            def load_unit(s, pair, src, tiles, cols):
                if not isinstance(pair, int) or pair > 0:
                    sp.wait_ge(w_lo_ready[s], pair)
                sp.dma_start(w_raw[:, s, 0:tiles * cols].rearrange("p (k n) -> p k n", k=tiles),
                             src).then_inc(w_loaded[s], 16)

            sp.dma_start(rows[:, 0, :].rearrange("j (h p) -> j h p", h=2),
                         lam_re[0].rearrange("(h j) p -> j h p", h=2)).then_inc(lam_loaded, 16)
            sp.dma_start(rows[:, 1, :].rearrange("j (h p) -> j h p", h=2),
                         lam_im[0].rearrange("(h j) p -> j h p", h=2)).then_inc(lam_loaded, 16)
            with nc.allow_non_contiguous_dma(reason="64 step sizes"):
                sp.dma_start(rows[:, 2, 0:2], log_step[0].rearrange("(h j) -> j h", h=2)).then_inc(lam_loaded, 16)
            sp.dma_start(ident[:, :], ident_in).then_inc(ident_loaded, 16)
            for ri, src in enumerate((b_re, b_im)):
                sp.dma_start(b_rows[:, ri, :].rearrange("j (h a) -> j h a", h=2),
                             src[0].rearrange("(h j) p n -> j h (p n)", h=2)).then_inc(b_loaded, 16)
            for half in range(2):
                gain_half = s5_norm[0][half * J * N:(half + 1) * J * N]
                sp.dma_start(gain_wide[64 * half:64 * half + 64, :], gain_half.partition_broadcast(64)).then_inc(gain_loaded, 16)
            for col, vec in ((V_GLU_B, glu_b[0]), (V_RET, ret_norm[0]), (V_FFN0, ffn_norm[0]),
                             (V_FFN1, ffn_norm[1]), (V_FINAL, final_norm), (V_GN, ret_gn[0])):
                n = vec.shape[0] // P
                sp.dma_start(vec_rows[col:col + n, :], vec.rearrange("(k p) -> k p", p=P)).then_inc(vecs_loaded, 16)
            for ri, src in enumerate((c_re, c_im)):
                for b in range(4):
                    sp.dma_start(c_rows[:, ri, b, :].rearrange("m (h p) -> m h p", h=2),
                                 src[0].rearrange("(h b j) n p -> b (j n) h p", h=2, b=4)[b]).then_inc(c_loaded, 16)
            for half in range(2):
                gain_half = s5_norm[0][half * J * N:(half + 1) * J * N]
                sp.dma_start(d_gain[N * half:N * half + N, :], gain_half.partition_broadcast(N)).then_inc(d_loaded, 16)
                sp.dma_start(d_diag[N * half:N * half + N, :, :],
                             s5_d[0][half * J:half * J + J, :].partition_broadcast(N)).then_inc(d_loaded, 16)
            for s in range(2):
                load_unit(s, 0, glu_v[:, :, 256 * s:256 * s + 256], KT, 256)
            b, fill = S5_AT[("tb", 2 * NBLK - 1)]
            sp.wait_ge(bank_full[b], fill + 1)
            sp.wait_ge(tb_ready, NBLK)
            sp.wait_ge(fb_ready, 4)
            sp.dma_start(x_tok, x[0].rearrange("(t p) d -> p t d", p=P)).then_inc(x_loaded, 16)
            sp.wait_ge(toep_zeroed, 8)
            for part in range(2):
                sp.wait_ge(diag_ready, part + 1)
                for half in range(2):
                    js = slice(J // 2 * part, J // 2 * part + J // 2)
                    gs = slice(J * half + J // 2 * part, J * half + J // 2 * part + J // 2)
                    for r in range(STEPS):
                        sp.dma_start(toep[N * r:N * r + N, gs, N * r:P],
                                     strip[N * half:N * half + N, js, 0:P - N * r]).then_inc(toep_loaded[part], 16)
            for s in range(2):
                load_unit(s, 1, glu_v[:, :, 512 + 256 * s:768 + 256 * s], KT, 256)

            def ffn_units(layer):
                with sp.Fori(0, HT) as i:
                    load_unit(0, i + PAIR0[f"ffn{layer}"], gate_v[layer][:, :, bass.ds(i * 256, 256)], KT, 256)
                    load_unit(1, i + PAIR0[f"ffn{layer}"], up_v[layer][:, :, bass.ds(i * 256, 256)], KT, 256)
                with sp.Fori(0, KT) as i:
                    for s in range(2):
                        load_unit(s, i + PAIR0[f"down{layer}"],
                                  down_v[layer][:, HT * s:HT * s + HT, bass.ds(i * P, P)], HT, P)

            ffn_units(0)
            sp.dma_start(rope[:, :, :], rope_in.rearrange("p (s a) -> p s a", s=2)).then_inc(rope_loaded, 16)
            with sp.Fori(0, H) as h:
                pair = h * 3 + PAIR0["ret"]
                load_unit(0, pair, ret_v[:, :, bass.ds(h * HD, HD)], KT, HD)
                load_unit(1, pair, ret_v[:, :, bass.ds(h * HD + D, HD)], KT, HD)
                for s in range(2):
                    load_unit(s, pair + 1, ret_v[:, 4 * s:4 * s + 4, bass.ds(h * VD + 2 * D, VD)], 4, VD)
                load_unit(0, pair + 2, ret_v[:, :, bass.ds(h * VD + 4 * D, 256)], KT, 256)
                sp.dma_start(decay, decay_in[:, bass.ds(h * SEQ, SEQ)]).then_inc(decay_loaded, 16)
                load_unit(1, pair + 2, ret_v[:, :, bass.ds(h * VD + 4 * D + 256, 256)], KT, 256)
            with sp.Fori(0, KT // 2) as i:
                for s in range(2):
                    load_unit(s, i + PAIR0["wo"], wo_v[:, :, bass.ds(i * 256 + P * s, P)], 2 * KT, P)
            ffn_units(1)
            for t in range(TT):
                sp.wait_ge(out_left, t + 1)
                sp.wait_ge(out_right, t + 1)
                sp.dma_start(out[0, t * P:t * P + P, :], out_sb[:, t, :]).then_inc(out_stored, 16)
            sp.wait_ge(out_stored, 16 * TT)

        @block.tensor
        def _(pe):
            def s5_open(kind, n):
                b, fill = S5_AT[(kind, n)]
                if fill:
                    pe.wait_ge(bank_free[b], fill)
                return bank[b], bank_full[b]

            def s5_tables(k):
                pe.wait_ge(tb_ready, k + 1)
                for ri in range(2):
                    ps, full = s5_open("tb", 2 * k + ri)
                    for j in range(JB):
                        mm = pe.transpose(ps[:, P * j:P * j + P], tb[:, k % 2, ri, P * j:P * j + P], ident[:, :])
                    mm.then_inc(full, 1)

            def s5_inputs(k):
                for ri in range(2):
                    b, fill = S5_AT[("tb", 2 * k + ri)]
                    pe.wait_ge(bank_free[b], fill + 1)
                ps, full = s5_open("b", k)
                for j in range(JB):
                    for ri in range(2):
                        for half in range(2):
                            jj = JB * k + j
                            col = (2 * j + ri) * CH
                            mm = pe.matmul(ps[64 * half:64 * half + 64, col:col + CH],
                                           tbt[:, jj, ri, 64 * half:64 * half + 64], u[:, J * half + jj, :],
                                           start=True, stop=True)
                mm.then_inc(full, 1)

            pe.wait_ge(ident_loaded, 16)
            pe.wait_ge(b_loaded, 32)
            for ri in range(2):
                ps, full = s5_open("bt", ri)
                for n in range(N):
                    mm = pe.transpose(ps[:, J * n:J * n + J], b_rows[:, ri, n::N], ident[0:J, 0:J])
                mm.then_inc(full, 1)
            ps, full = s5_open("vec", 0)
            pe.wait_ge(vecs_loaded, 6 * 16)
            pe.transpose(ps[:, 0:NVEC], vec_rows, ident[64:64 + NVEC, 64:64 + NVEC]).then_inc(full, 1)
            ps, full = s5_open("lam", 0)
            pe.wait_ge(rows_ready, 1)
            for i in range(4):
                mm = pe.transpose(ps[:, J * i:J * i + J], rows[:, 3 + i, :], ident[0:J, 0:J])
            mm.then_inc(full, 1)
            pe.wait_ge(c_loaded, 8 * 16)
            for ri in range(2):
                ps, full = s5_open("ct", ri)
                for b in range(4):
                    mm = pe.transpose(ps[:, P * b:P * b + P], c_rows[:, ri, b, :], ident[:, :])
                mm.then_inc(full, 1)
            s5_tables(0)
            pe.wait_ge(xn_ready, STEPS)
            for k in range(8):
                if k == 5:
                    s5_tables(1)
                ps, full = s5_open("u", k)
                for i in range(8):
                    mm = pe.transpose(ps[:, CH * i:CH * i + CH],
                                      xn[:, 8 * k + i, :, :].rearrange("p t n -> p (t n)"), ident[64:128, 64:128])
                mm.then_inc(full, 1)
            for k in range(8):
                b, fill = S5_AT[("u", k)]
                pe.wait_ge(bank_free[b], fill + 1)
            s5_inputs(0)
            for k in range(2, NBLK):
                s5_tables(k)
                s5_inputs(k - 1)
            s5_inputs(NBLK - 1)
            pe.wait_ge(fb_ready, 4)
            def strips(k):
                pe.wait_ge(tc_ready, k + 1)
                ps, full = s5_open("strip", k)
                for i in range(JB):
                    for ri in range(2):
                        mm = pe.matmul(ps[0:2 * N, P * i:P * i + P], fb[:, ri, JB * k + i, :],
                                       r_tc[:, ri, JB * k + i, :, :], start=(ri == 0), stop=(ri == 1))
                mm.then_inc(full, 1)

            for k in range(6):
                strips(k)
            pe.wait_ge(x_loaded, 16)
            for k in range(KT):
                ps, full = s5_open("xt", k)
                for t in range(TT):
                    mm = pe.transpose(ps[:, P * t:P * t + P], x_tok[:, t, P * k:P * k + P], ident[:, :])
                mm.then_inc(full, 1)
            for k in range(6, NBLK):
                strips(k)

            def y_pairs(k):
                for i in range(4):
                    for half in range(2):
                        rows64 = slice(64 * half, 64 * half + 64)
                        yield 4 * k + i, half, rows64, bank[S5_AT[("y", k)][0]][rows64, P * i:P * i + P]

            def y_states(k):
                if k % 4 == 0:
                    pe.wait_ge(scan_step[k // 4], 3 * (CH - 1))
                for jj, half, rows64, o in y_pairs(k):
                    for ri in range(2):
                        mm = pe.matmul(o, states[rows64, 0:CH, ri, jj], r_tc[rows64, ri, jj, :, :],
                                       start=False, stop=(jj % 4 == 3 and ri == 1))
                mm.then_inc(bank_full[S5_AT[("y", k)][0]], 1)

            def y_transposed(k):
                if k % 2 == 0:
                    b, fill = S5_AT[("y", k + 1)]
                    pe.wait_ge(bank_free[b], fill + 1)
                ps, full = s5_open("yt", k)
                for i in range(4):
                    mm = pe.transpose(ps[:, P * i:P * i + P], y_chunk[:, k // 2 % 2, 4 * (k % 2) + i, :], ident[:, :])
                mm.then_inc(full, 1)

            for k in range(8):
                if k % 4 == 0:
                    pe.wait_ge(toep_loaded[k // 4], 16 * 2 * STEPS)
                s5_open("y", k)
                for jj, half, rows64, o in y_pairs(k):
                    pe.matmul(o, u[:, J * half + jj, :], toep[:, J * half + jj, :], start=(jj % 4 == 0), stop=False)
            for k in range(8):
                y_states(k)
                if k >= 3 and k % 2:
                    y_transposed(k - 3)
                    y_transposed(k - 2)
            y_transposed(6)
            y_transposed(7)

            def product(o, w, w_cols, hi, lo, first, end):
                pe.matmul(o, w_hi[w][:, w_cols], hi, start=first, stop=False)
                pe.matmul(o, w_hi[w][:, w_cols], lo, start=False, stop=False)
                return pe.matmul(o, w_lo[w][:, w_cols], hi, start=False, stop=end)

            def open_bank(b, fill):
                pe.wait_ge(bank_free[b], fill)

            def two_tiles(s, pair, banks, fills, split, split0):
                glu = split is y_split
                hi, lo = (g_hi, g_lo) if glu else (u_hi, u_lo)
                pe.wait_ge(w_lo_ready[s], pair + 1)
                for b, fill in zip(banks, fills):
                    open_bank(b, fill)
                for n in range(KT):
                    k = n // 2 + KT // 2 * (n % 2) if glu else n
                    if glu and n % 2 == 0:
                        pe.wait_ge(y_split, n // 2 + 1)
                    elif split is not None and not glu:
                        pe.wait_ge(split, split0 + n + 1)
                    for m, b in enumerate(banks):
                        cols = slice(256 * k + P * m, 256 * k + P * m + P)
                        mm = product(bank[b][:, :], s, cols, hi[:, k, :], lo[:, k, :], n == 0, n == KT - 1)
                        if n == KT - 1 and m == 0:
                            mm.then_inc(bank_full[b], 1)
                mm.then_inc(w_used[s], 1)

            def rms_sum(norm):
                b0 = FREE0[f"norm{norm}"][7]
                pe.wait_ge(sum_done, (KT + 1) * (norm + 1))
                open_bank(7, b0)
                pe.matmul(bank[7][:, :], ones[:, :], sq_sum, start=True, stop=True).then_inc(bank_full[7], 1)

            def rms_columns(b, fill):
                open_bank(b, fill)
                for t in range(TT):
                    mm = pe.matmul(bank[b][:, t:t + 1], sq_sum[:, P * t:P * t + P], ones[:, 0:1], start=True, stop=True)
                mm.then_inc(bank_full[b], 1)

            with pe.Fori(0, 2) as i:
                for s in range(2):
                    banks = [2 * s, 2 * s + 1]
                    two_tiles(s, i + PAIR0["glu"], banks, [i + FREE0["glu"][b] for b in banks], y_split, 0)

            def ffn_products(layer, norm):
                def hidden_tiles(i, s, split):
                    banks = [2 * s, 2 * s + 1]
                    two_tiles(s, i + PAIR0[f"ffn{layer}"], banks, [i + FREE0[f"ffn{layer}"][b] for b in banks],
                              split, KT * norm)

                hidden_tiles(0, 0, u_split)
                rms_sum(norm)
                hidden_tiles(0, 1, None)
                with pe.Fori(1, HT) as i:
                    for s in range(2):
                        hidden_tiles(i, s, None)
                with pe.Fori(0, KT // 2) as i:
                    for m in range(2):
                        b = 4 + m
                        open_bank(b, i + FREE0[f"down{layer}"][b])
                        for s in range(2):
                            pe.wait_ge(w_lo_ready[s], i * 2 + PAIR0[f"down{layer}"] + m + 1)
                            for k in range(HT):
                                kk = HT * s + k
                                pe.wait_ge(h_split, FT * layer + kk + 1)
                                mm = product(bank[b][:, :], s, slice(P * k, P * k + P), h_hi[:, kk, :],
                                             h_lo[:, kk, :], kk == 0, kk == FT - 1)
                            mm.then_inc(w_used[s], 1)

            ffn_products(0, 0)

            rms_sum(1)
            rms_columns(6, FREE0["norm1"][6])
            with pe.Fori(0, H) as h:
                pair = h * 3 + PAIR0["ret"]
                fill = [h * 3 + FREE0["ret"][b] for b in range(8)]
                two_tiles(0, pair, [0, 1], fill[0:2], u_split, 8)
                two_tiles(1, pair, [2, 3], fill[2:4], None, 0)
                for s in range(2):
                    pe.wait_ge(w_lo_ready[s], pair + 2)
                    for t in range(TT):
                        if s == 0:
                            open_bank(4 + t, fill[4 + t])
                        for k in range(4):
                            kk = 4 * s + k
                            cols = slice(VD * k, VD * k + VD)
                            a_hi, a_lo = u_hi[:, kk, P * t:P * t + P], u_lo[:, kk, P * t:P * t + P]
                            o = bank[4 + t][:, :]
                            pe.matmul(o, a_hi, w_hi[s][:, cols], start=(kk == 0), stop=False)
                            pe.matmul(o, a_hi, w_lo[s][:, cols], start=False, stop=False)
                            mm = pe.matmul(o, a_lo, w_hi[s][:, cols], start=False, stop=(kk == KT - 1))
                        if s == 1 and t < TT - 1:
                            mm.then_inc(bank_full[4 + t], 1)
                    mm.then_inc(w_used[s], 1)
                pe.wait_ge(rope_ready, h * 2 + 2)
                for jt in range(TT):
                    open_bank(jt, fill[jt] + 1)
                    for d in range(2):
                        mm = pe.matmul(bank[jt][:, 0:SEQ - P * jt], qk[:, 2 + d, P * jt:P * jt + P],
                                       qk[:, d, P * jt:SEQ], start=(d == 0), stop=(d == 1))
                    mm.then_inc(bank_full[jt], 1)
                two_tiles(0, pair + 2, [4, 5], [f + 1 for f in fill[4:6]], None, 0)
                for t in range(TT):
                    open_bank(4 + t, fill[4 + t] + 1)
                for t in range(TT):
                    open_bank(t, fill[t] + 2)
                for it in range(TT):
                    for jt in range(it + 1):
                        mm = pe.matmul(bank[it][:, :], scores[jt][:, P * (it - jt):P * (it - jt) + P], v[:, jt, :],
                                       start=(jt == 0), stop=(jt == it))
                    mm.then_inc(bank_full[it], 1)
                two_tiles(1, pair + 2, [6, 7], [f + 1 for f in fill[6:8]], None, 0)
                for m in range(4):
                    open_bank(4 + m, fill[4 + m] + 2)
                    for it in range(TT):
                        if m == 0:
                            open_bank(it, fill[it] + 3)
                        mm = pe.transpose(bank[4 + m][:, P * it:P * it + P], o_norm[:, it, P * m:P * m + P], ident[:, :])
                    mm.then_inc(bank_full[4 + m], 1)
            with pe.Fori(0, KT // 2) as i:
                for s in range(2):
                    pe.wait_ge(w_lo_ready[s], i + PAIR0["wo"] + 1)
                    open_bank(s, i + FREE0["wo"][s])
                    for k in range(4 * H):
                        pe.wait_ge(ret_split, k + 1)
                        mm = product(bank[s][:, :], s, slice(P * k, P * k + P), y_hi[:, k, :], y_lo[:, k, :],
                                     k == 0, k == 4 * H - 1)
                    mm.then_inc(w_used[s], 1)
            ffn_products(1, 2)

            def transposed_steps(t):
                for half in range(2):
                    b = 2 * t + half
                    open_bank(b, FREE0["store"][b])
                    for k in range(4):
                        kk = 4 * half + k
                        pe.wait_ge(final_ready, kk + 1)
                        mm = pe.transpose(bank[b][:, P * k:P * k + P], final[:, kk, P * t:P * t + P], ident[:, :])
                    mm.then_inc(bank_full[b], 1)

            for t in range(TT - 1):
                transposed_steps(t)
            pe.wait_ge(sum_done, (KT + 1) * 4)
            rms_columns(7, FREE0["norm3"][7])
            transposed_steps(TT - 1)

        @block.scalar
        def _(act):
            def s5_full(kind, n):
                b, fill = S5_AT[(kind, n)]
                act.wait_ge(bank_full[b], fill + 1)
                return bank[b], bank_free[b]

            def copy(o, i, scale=1.0):
                return act.activation(o, i, ACT.Copy, scale=scale)

            def split_weights(s, pair):
                act.wait_ge(w_loaded[s], (pair + 1) * 16)
                if not isinstance(pair, int) or pair > 0:
                    act.wait_ge(w_used[s], pair)
                copy(w_hi[s][:, :], w_raw[:, s, :]).then_inc(w_hi_ready[s], 1)

            act.dma_start(xc, x[0].rearrange("(c t) d -> c t d", t=STEPS)).then_inc(xc_loaded, 16)
            for ri in range(2):
                ps, free = s5_full("bt", ri)
                copy(bt[:, ri, :, :].rearrange("p j n -> p n j"),
                     ps[:, :].rearrange("p (n j) -> p n j", n=N)).then_inc(free, 1)
            act.wait_ge(xc_loaded, 16)

            def chunk_squares(t0, t1):
                for t in range(t0, t1):
                    if t:
                        act.wait_ge(ms_ready, t)
                    act.activation(junk, xc[:, t, :], ACT.Square, accum_out=small[0:64, t:t + 1]).then_inc(ms_ready, 1)

            chunk_squares(0, 2)
            act.wait_ge(phase_ready, 1)
            act.activation(rows[:, 11, :], rows[:, 10, :], ACT.Sin).then_inc(sin_ready, 1)
            act.activation(rows[:, 12, :], rows[:, 10, :], ACT.Sin, scale=0.5).then_inc(sin_ready, 1)
            chunk_squares(2, STEPS)
            ps, free = s5_full("vec", 0)
            copy(vecs[:, :], ps[:, 0:NVEC]).then_inc(free, 1)
            ps, free = s5_full("lam", 0)
            copy(lam_t[:, :, :].rearrange("p i j -> p (i j)"), ps[:, 0:4 * J]).then_inc(free, 1)
            act.wait_ge(ms_ready, STEPS)
            act.wait_ge(consts_set, 1)
            act.activation(small[0:64, 8:16], small[0:64, 0:8], ACT.Sqrt, bias=eps[0:64, :],
                           scale=1.0 / D).then_inc(rms_ready, 1)
            for ri in range(2):
                ps, free = s5_full("ct", ri)
                copy(ct[:, ri, :, :].rearrange("p j n -> p (j n)"), ps[:, :], -1.0 if ri else 1.0).then_inc(free, 1)
            act.wait_ge(rs_ready, 1)
            for t in range(STEPS):
                act.activation(xn[:, :, t, :], xc[:, t, :].rearrange("p (g n) -> p g n", g=G), ACT.Copy,
                               scale=small[0:64, 16 + t:17 + t]).then_inc(xn_ready, 1)

            def s5_table_out(k):
                for ri in range(2):
                    ps, free = s5_full("tb", 2 * k + ri)
                    copy(tbt[:, JB * k:JB * k + JB, ri, :], ps[:, :].rearrange("p (j m) -> p j m", j=JB)).then_inc(free, 1)

            def s5_input_out(k):
                ps, free = s5_full("b", k)
                copy(states[:, 1:CH + 1, :, JB * k:JB * k + JB].rearrange("p c r j -> p j r c"),
                     ps[:, :].rearrange("p (j r c) -> p j r c", j=JB, r=2)).then_inc(free, 1)

            def zero_toeplitz(k):
                act.activation(toep[:, 8 * k:8 * k + 8, :].rearrange("p g m -> p (g m)"),
                               eps[:, :].broadcast_to([P, 8 * P]), ACT.Copy, scale=0.0).then_inc(toep_zeroed, 1)

            s5_table_out(0)
            for k in range(8):
                if k == 5:
                    s5_table_out(1)
                ps, free = s5_full("u", k)
                copy(u[:, 8 * k:8 * k + 8, :], ps[:, :].rearrange("p (g c) -> p g c", g=8)).then_inc(free, 1)
            s5_input_out(0)
            for k in range(2, NBLK):
                s5_table_out(k)
                s5_input_out(k - 1)
                zero_toeplitz(k - 2)
            s5_input_out(NBLK - 1)
            for k in range(6, 8):
                zero_toeplitz(k)

            def strip_out(k):
                ps, free = s5_full("strip", k)
                copy(strip[:, JB * k:JB * k + JB, :].rearrange("p j m -> p (j m)"), ps[0:2 * N, :]).then_inc(free, 1)

            for k in range(6):
                strip_out(k)
            for k in range(KT):
                ps, free = s5_full("xt", k)
                copy(xT[:, k, :], ps[:, :]).then_inc(free, 1)
            for k in range(6, NBLK):
                strip_out(k)
            split_weights(0, 0)

            def gelu(k):
                ps, free = s5_full("y", k)
                if k >= 4:
                    b, fill = S5_AT[("yt", 2 * (k // 2) - 3)]
                    act.wait_ge(bank_full[b], fill + 1)
                at = 64 * (k % 2)
                act.activation(y_chunk[:, k // 2 % 2, :, at:at + 64].rearrange("p t (j n) -> p j t n", j=4),
                               ps[:, :].rearrange("p (j t n) -> p j t n", j=4, t=STEPS),
                               ACT.Gelu_apprx_tanh).then_inc(free, 1)

            def y_high(jb):
                b, fill = S5_AT[("yt", 2 * jb + 1)]
                act.wait_ge(bank_free[b], fill + 1)
                copy(g_hi[:, jb:jb + 5:4, :], y_raw[:, jb % 2, :, :]).then_inc(y_hi_ready, 1)

            for k in range(8):
                gelu(k)
                if k >= 5 and k % 2:
                    y_high((k - 5) // 2)
            for jb in range(2, 4):
                y_high(jb)
            split_weights(1, 0)

            def square(t):
                act.activation(sq, tile(xT, t), ACT.Square).then_inc(sq_ready, 1)

            def u_high(i, t, m):
                act.wait_ge(u_raw_ready, t + (KT * i + 1))
                copy(tile(u_hi, t), act_raw[:, m, :]).then_inc(u_hi_ready, 1)

            def root(i):
                b = FULL0[f"norm{i}"][7]
                act.wait_ge(bank_full[7], b + 1)
                act.activation(rs, bank[7][:, :], ACT.Sqrt, bias=eps[:, :], scale=1.0 / D).then_inc(bank_free[7], 1)

            def root_columns(b, norm):
                act.wait_ge(bank_full[b], FULL0[norm][b] + 1)
                act.activation(rms_col, bank[b][:, 0:TT], ACT.Sqrt, bias=eps[:, :], scale=1.0 / D).then_inc(bank_free[b], 1)

            with act.Fori(0, 2) as i:
                for m in range(4):
                    if m % 2:
                        act.wait_ge(w_used[m // 2], i + PAIR0["glu"] + 1)
                    else:
                        act.wait_ge(bank_full[m], i + FULL0["glu"][m] + 1)
                    act.activation(sig[:, m % 2, :], bank[m][:, :], ACT.Sigmoid,
                                   bias=vecs[:, bass.ds(i * 4 + V_GLU_B + m, 1)]).then_inc(bank_free[m], 1)
                    if m % 2:
                        split_weights(m // 2, i + PAIR0["glu"] + 1)
                    act.wait_ge(x_new, i * 4 + m + 1)
                    square(i * 4 + m)
                    u_high(0, i * 4 + m, m % 2)
            root(0)

            def ffn(layer, i_norm):
                def body(i, last_of_all):
                    for m in range(2):
                        pair = i * 2 + m + PAIR0[f"down{layer}"]
                        if not (last_of_all and m == 1):
                            split_weights(0, pair + 1)
                        act.wait_ge(bank_free[4 + m], i + FREE0[f"down{layer}"][4 + m] + 1)
                        square(i * 2 + m)
                        if i_norm < 3:
                            u_high(i_norm, i * 2 + m, m)
                        if not (last_of_all and m == 1):
                            split_weights(1, pair + 1)

                with act.Fori(0, HT) as i:
                    pair = i + PAIR0[f"ffn{layer}"]
                    for m in range(2):
                        act.wait_ge(bank_free[m], i + FREE0[f"ffn{layer}"][m] + 1)
                        act.activation(sig[:, m, :], sig[:, m, :], ACT.Silu).then_inc(gate_ready, 1)
                    split_weights(0, pair + 1)
                    for m in range(2):
                        act.wait_ge(h_raw_ready, i * 2 + (FT * layer + m + 1))
                        copy(tile(h_hi, i * 2 + m), act_raw[:, m, :]).then_inc(h_hi_ready, 1)
                    split_weights(1, pair + 1)
                if layer == 0:
                    with act.Fori(0, KT // 2) as i:
                        body(i, False)
                else:
                    with act.Fori(0, KT // 2 - 1) as i:
                        body(i, False)
                    body(KT // 2 - 1, True)

            ffn(0, 1)
            root(1)
            root_columns(6, "norm1")
            def silu_gate(free, m):
                act.wait_ge(bank_free[4 + m], free[4 + m] + 2)
                act.activation(gate[:, m, :], gate[:, m, :], ACT.Silu).then_inc(gate_ready, 1)

            act.wait_ge(rs_col_ready, 1)
            with act.Fori(0, H) as h:
                pair = h * 3 + PAIR0["ret"]
                free = [h * 3 + FREE0["ret"][b] for b in range(8)]
                for p in range(2):
                    for s in range(2):
                        split_weights(s, pair + p + 1)
                for t in range(TT):
                    if t < TT - 1:
                        n = 2 if t == 1 else 3
                        act.wait_ge(bank_full[4 + t], h * n + FULL0["ret"][4 + t] + 1)
                    else:
                        act.wait_ge(w_used[1], pair + 2)
                    act.activation(v[:, t, :], bank[4 + t][:, :], ACT.Copy,
                                   scale=rs_col[:, t:t + 1]).then_inc(bank_free[4 + t], 1)
                split_weights(0, pair + 3)
                for m in range(2):
                    silu_gate(free, m)
                act.wait_ge(var_ready, h + 1)
                act.activation(o_std[:, :], moments[:, :, 1], ACT.Sqrt, bias=eps[:, :]).then_inc(std_ready, 1)
                split_weights(1, pair + 3)
                for m in range(2):
                    silu_gate(free, 2 + m)
                for m in range(4):
                    act.wait_ge(bank_free[4 + m], free[4 + m] + 3)
                    copy(tile(y_hi, h * 4 + m), act_raw[:, m % 2, :]).then_inc(ret_hi_ready, 1)
            with act.Fori(0, KT // 2) as i:
                for s in range(2):
                    act.wait_ge(bank_free[s], i + FREE0["wo"][s] + 1)
                    square(i * 2 + s)
                    u_high(2, i * 2 + s, s)
                    split_weights(s, i + PAIR0["wo"] + 1)
            root(2)
            ffn(1, 3)
            root_columns(7, "norm3")
            act.wait_ge(rs_col_ready, 2)
            for t in range(TT):
                act.wait_ge(bank_full[2 * t], FULL0["store"][2 * t] + 1)
                act.activation(out_sb[:, t, 0:512], bank[2 * t][:, :], ACT.Copy,
                               scale=rs_col[:, t:t + 1]).then_inc(out_left, 1)

        @block.vector
        def _(dve):
            steps = [0]

            def step(ins):
                steps[0] += 1
                return ins.then_inc(dve_step, 1)

            def settle():
                dve.wait_ge(dve_step, steps[0])

            def mul(o, a, b):
                return dve.tensor_tensor(o, a, b, ALU.mult)

            def s5_full(kind, n):
                b, fill = S5_AT[(kind, n)]
                dve.wait_ge(bank_full[b], fill + 1)
                return bank[b], bank_free[b]

            def split_weights(s, pair):
                dve.wait_ge(w_hi_ready[s], pair + 1)
                dve.tensor_tensor(w_lo[s][:, :], w_raw[:, s, :], w_hi[s][:, :].bitcast(F32),
                                  ALU.subtract).then_inc(w_lo_ready[s], 1)

            step(dve.memset(eps[:, :], EPS))
            settle()
            dve.memset(ones[:, :], 1.0).then_inc(consts_set, 1)

            def exp(o, i, t0, t1, t2):
                magic = 12582912.0
                step(dve.tensor_scalar(t0, i, -87.0, 88.0, ALU.max, ALU.min))
                settle()
                step(dve.tensor_scalar(t1, t0, 1.4426950408889634, magic, ALU.mult, ALU.add))
                settle()
                step(dve.tensor_scalar(t1, t1, magic, None, ALU.subtract))
                settle()
                for c in (-0.693359375, 2.12194440e-4):
                    step(dve.scalar_tensor_tensor(out=t0, in0=t1, scalar=c, in1=t0, op0=ALU.mult, op1=ALU.add))
                    settle()
                step(dve.tensor_scalar(t2, t0, 1.0 / 5040, None, ALU.mult))
                settle()
                for n in (720, 120, 24, 6, 2, 1):
                    step(dve.scalar_tensor_tensor(out=t2, in0=t2, scalar=1.0 / n, in1=t0, op0=ALU.add, op1=ALU.mult))
                    settle()
                step(dve.tensor_scalar(o.bitcast(I32), t1, 127.0, 8388608.0, ALU.add, ALU.mult))
                settle()
                step(dve.scalar_tensor_tensor(out=o, in0=t2, scalar=1.0, in1=o, op0=ALU.add, op1=ALU.mult))
                settle()

            def row(n, w=P):
                return rows[:, n, 0:w]

            dve.wait_ge(lam_loaded, 48)
            exp(row(7, 2), row(2, 2), row(8, 2), row(9, 2), row(13, 2))
            for half in range(2):
                cols = slice(ST * half, ST * half + ST)
                for i in range(2):
                    step(dve.tensor_scalar(rows[:, 14 + i, cols], rows[:, i, cols], rows[:, 7, half:half + 1], None,
                                           ALU.mult))
            settle()
            two_pi = 2 * np.pi
            c1 = 6.28125
            c2 = float(np.float32(round((two_pi - c1) * 2**21) / 2**21))
            c3 = float(np.float32(two_pi - c1 - c2))
            step(dve.tensor_scalar(row(8), row(15), 1.0 / two_pi, 12582912.0, ALU.mult, ALU.add))
            settle()
            step(dve.tensor_scalar(row(8), row(8), 12582912.0, None, ALU.subtract))
            settle()
            a = row(15)
            for c in (c1, c2, c3):
                step(dve.scalar_tensor_tensor(out=row(9), in0=row(8), scalar=-c, in1=a, op0=ALU.mult, op1=ALU.add))
                settle()
                a = row(9)
            dve.tensor_scalar(row(10), row(9), -3.1415925, 3.1415925, ALU.max, ALU.min).then_inc(phase_ready, 1)
            exp(row(7), row(14), row(8), row(13), row(16))
            dve.wait_ge(sin_ready, 2)
            step(mul(row(17), row(12), row(12)))
            settle()
            step(dve.tensor_scalar(row(17), row(17), -2.0, 1.0, ALU.mult, ALU.add))
            settle()
            step(mul(row(3), row(7), row(17)))
            step(mul(row(4), row(7), row(11)))
            step(mul(row(18), row(0), row(0)))
            step(mul(row(19), row(1), row(1)))
            settle()
            step(dve.tensor_tensor(row(18), row(18), row(19), ALU.add))
            step(dve.tensor_scalar(row(20), row(3), 1.0, None, ALU.subtract))
            settle()
            step(dve.reciprocal(row(18), row(18)))
            step(mul(row(21), row(20), row(0)))
            step(mul(row(22), row(4), row(1)))
            step(mul(row(23), row(4), row(0)))
            step(mul(row(24), row(20), row(1)))
            settle()
            step(dve.tensor_tensor(row(21), row(21), row(22), ALU.add))
            step(dve.tensor_tensor(row(23), row(23), row(24), ALU.subtract))
            settle()
            step(mul(row(5), row(21), row(18)))
            mul(row(6), row(23), row(18)).then_inc(rows_ready, 1)

            def complex_mul(o, a, b, t):
                step(mul(t[0], a, repeated(b[0], 1, 2)))
                step(mul(t[1], a, repeated(b[1], 1, 2)))
                settle()
                step(dve.tensor_tensor(o[0], t[0][:, 0], t[1][:, 1], ALU.subtract))
                step(dve.tensor_tensor(o[1], t[0][:, 1], t[1][:, 0], ALU.add))
                settle()

            step(dve.memset(powers[:, 0, 0, :], 1.0))
            step(dve.memset(powers[:, 1, 0, :], 0.0))
            dve.wait_ge(gain_loaded, 32)
            for ri in range(2):
                b, fill = S5_AT[("bt", ri)]
                dve.wait_ge(bank_free[b], fill + 1)
                b_flat = bt[:, ri, :, :].rearrange("p j n -> p (j n)")
                mul(b_flat, b_flat, gain_wide).then_inc(bt_ready, 1)
            b, fill = S5_AT[("lam", 0)]
            dve.wait_ge(bank_free[b], fill + 1)
            step(dve.tensor_copy(powers[:, :, 1, :], lam_t[:, 0:2, :]))
            settle()
            for have in (1, 2, 4):
                t = [prod[:, i, 0:2 * have * J].rearrange("p (r k j) -> p r k j", r=2, k=have) for i in range(2)]
                top = [repeated(powers[:, i, have, :], 1, have) for i in range(2)]
                complex_mul([powers[:, i, have + 1:2 * have + 1, :] for i in range(2)],
                            powers[:, :, 1:have + 1, :], top, t)
            dve.wait_ge(rms_ready, 1)
            dve.reciprocal(small[0:64, 16:24], small[0:64, 8:16]).then_inc(rs_ready, 1)
            t = [prod[:, i, :].rearrange("p (r k j) -> p r k j", r=2, k=STEPS) for i in range(2)]
            complex_mul([b_powers[:, i, :, :] for i in range(2)], powers[:, :, 1:STEPS + 1, :][:, :, ::-1, :],
                        [repeated(lam_t[:, 2 + i, :], 1, STEPS) for i in range(2)], t)
            step(dve.tensor_copy(step8[:, 0, :, :], repeated(powers[:, 0, STEPS, :], 1, 2)))
            step(dve.tensor_copy(step8[:, 1, 0, :], powers[:, 1, STEPS, :]))
            dve.tensor_scalar(step8[:, 1, 1, :], powers[:, 1, STEPS, :], -1.0, None, ALU.mult).then_inc(powers_ready, 1)
            dve.wait_ge(powers_ready, 1)

            def tables(k):
                js = slice(JB * k, JB * k + JB)
                if k >= 2:
                    b, fill = S5_AT[("tb", 2 * k - 3)]
                    dve.wait_ge(bank_full[b], fill + 1)
                t = [prod[:, i, :].rearrange("p (j t n) -> p j t n", j=JB, t=STEPS) for i in range(2)]

                def two(b_first, o, op):
                    for i in range(2):
                        step(mul(t[i], repeated(bt[:, i, js, :], 2, STEPS),
                                 repeated(b_powers[:, i ^ b_first, :, js].rearrange("p t j -> p j t"), 3, N)))
                    settle()
                    return dve.tensor_tensor(o, prod[:, 0, :], prod[:, 1, :], op)

                step(two(0, tb[:, k % 2, 0, :], ALU.subtract))
                settle()
                two(1, tb[:, k % 2, 1, :], ALU.add).then_inc(tb_ready, 1)
                dve.wait_ge(tb_ready, k + 1)

            dve.wait_ge(bt_ready, 2)
            for k in range(NBLK):
                tables(k)

            dve.wait_ge(state0_ready, 1)

            def inputs_ready(part):
                for k in range(NBLK // 2 * part, NBLK // 2 * part + NBLK // 2):
                    b, fill = S5_AT[("b", k)]
                    dve.wait_ge(bank_free[b], fill + 1)

            inputs_ready(0)
            JH, LAG = J // 2, 7
            for k in range(1, CH + LAG):
                turn = [(part, k - LAG * part) for part in range(2) if 0 < k - LAG * part < CH]
                for op in range(3):
                    for part, n in turn:
                        js = slice(JH * part, JH * part + JH)
                        if part and n == 1 and op == 0:
                            inputs_ready(1)
                        if n > 1 or op:
                            dve.wait_ge(scan_step[part], 3 * (n - 1) + op)
                        after, t = states[:, n + 1, :, js], scan_tmp[:, :, :, js]
                        if op == 0:
                            ins = mul(t, repeated(states[:, n, :, js], 1, 2), step8[:, :, :, js])
                        else:
                            ins = dve.tensor_tensor(after, after, t[:, 1, ::-1, :] if op == 2 else t[:, 0, :, :], ALU.add)
                        ins.then_inc(scan_step[part], 1)
            for part in range(2):
                dve.wait_ge(scan_step[part], 3 * (CH - 1))

            split_weights(0, 0)

            def y_copy(k):
                ps, free = s5_full("yt", k)
                if k >= 4 and k % 2 == 0:
                    dve.wait_ge(y_split, k // 2 - 1)
                dve.tensor_copy(y_raw[:, k // 2 % 2, :, :].rearrange("p h (c t) -> p t h c", t=STEPS)[
                    :, 4 * (k % 2):4 * (k % 2) + 4], ps[:, :].rearrange("p (t h c) -> p t h c", t=4, h=2)
                                ).then_inc(free, 1)

            def y_low(jb):
                dve.wait_ge(y_hi_ready, jb + 1)
                dve.tensor_tensor(g_lo[:, jb:jb + 5:4, :], y_raw[:, jb % 2, :, :],
                                  g_hi[:, jb:jb + 5:4, :].bitcast(F32), ALU.subtract).then_inc(y_split, 1)

            for jb in range(4):
                y_copy(2 * jb)
                y_copy(2 * jb + 1)
                if jb:
                    y_low(jb - 1)
            y_low(3)
            split_weights(1, 0)

            def clear_sum():
                dve.memset(sq_sum, 0.0).then_inc(sum_done, 1)

            def add_square(i, t):
                dve.wait_ge(sq_ready, t + (KT * i + 1))
                dve.wait_ge(sum_done, t + ((KT + 1) * i + 1))
                dve.tensor_tensor(sq_sum, sq_sum, sq, ALU.add).then_inc(sum_done, 1)

            def add_to_x(t, a):
                return dve.tensor_tensor(tile(xT, t), a, tile(xT, t), ALU.add)

            def gained(i, t, m, gain_col):
                if i == 3:
                    o, ready = tile(final, t), final_ready
                else:
                    o, ready = act_raw[:, m, :], u_raw_ready
                dve.tensor_scalar(o, tile(xT, t), vecs[:, bass.ds(t + gain_col, 1)], None, ALU.mult).then_inc(ready, 1)

            def u_low(i, t, m):
                dve.wait_ge(u_hi_ready, t + (KT * i + 1))
                dve.tensor_tensor(tile(u_lo, t), act_raw[:, m, :], tile(u_hi, t).bitcast(F32),
                                  ALU.subtract).then_inc(u_split, 1)

            def inverse_rms(i):
                dve.wait_ge(bank_free[7], FREE0[f"norm{i}"][7] + 1)
                dve.reciprocal(rs, rs).then_inc(rs_done, 1)
                dve.wait_ge(rs_done, i + 1)

            def inverse_columns(b, norm, n):
                dve.wait_ge(bank_free[b], FREE0[norm][b] + 1)
                dve.reciprocal(rs_col, rms_col).then_inc(rs_col_ready, 1)
                dve.wait_ge(rs_col_ready, n)

            clear_sum()
            with dve.Fori(0, 2) as i:
                for m in range(4):
                    t = i * 4 + m
                    dve.tensor_tensor(y_whole, tile(g_hi, t).bitcast(F32), tile(g_lo, t).bitcast(F32),
                                      ALU.add).then_inc(glu_ready, 1)
                    dve.wait_ge(glu_ready, i * 8 + (2 * m + 1))
                    dve.wait_ge(bank_free[m], i + FREE0["glu"][m] + 1)
                    mul(y_whole, sig[:, m % 2, :], y_whole).then_inc(glu_ready, 1)
                    dve.wait_ge(glu_ready, i * 8 + (2 * m + 2))
                    add_to_x(t, y_whole).then_inc(x_new, 1)
                    dve.wait_ge(x_new, i * 4 + (m + 1))
                    if m >= 2:
                        dve.wait_ge(u_split, i * 4 + (m - 1))
                    gained(0, t, m % 2, V_FFN0)
                    add_square(0, i * 4 + m)
                    u_low(0, t, m % 2)
                    if m % 2:
                        split_weights(m // 2, i + PAIR0["glu"] + 1)
                dve.wait_ge(u_split, i * 4 + 4)
            inverse_rms(0)

            def ffn(layer, i_norm, gain_col):
                def body(i, last_of_all):
                    for m in range(2):
                        pair = i * 2 + m + PAIR0[f"down{layer}"]
                        if not (last_of_all and m == 1):
                            split_weights(0, pair + 1)
                        dve.wait_ge(w_used[1], pair + 1)
                        add_to_x(i * 2 + m, bank[4 + m][:, :]).then_inc(bank_free[4 + m], 1)
                        dve.wait_ge(bank_free[4 + m], i + (FREE0[f"down{layer}"][4 + m] + 1))
                        gained(i_norm, i * 2 + m, m, gain_col)
                        add_square(i_norm, i * 2 + m)
                        if i_norm < 3:
                            u_low(i_norm, i * 2 + m, m)
                        if not (last_of_all and m == 1):
                            split_weights(1, pair + 1)
                    if i_norm < 3:
                        dve.wait_ge(u_split, i * 2 + (KT * i_norm + 2))

                gates0 = (FT + 4 * H) * layer
                with dve.Fori(0, HT) as i:
                    pair = i + PAIR0[f"ffn{layer}"]
                    for m in range(2):
                        if m:
                            dve.wait_ge(w_used[0], pair + 1)
                        else:
                            dve.wait_ge(bank_full[0], i + FULL0[f"ffn{layer}"][0] + 1)
                        dve.tensor_tensor(sig[:, m, :], bank[m][:, :], rs, ALU.mult).then_inc(bank_free[m], 1)
                    split_weights(0, pair + 1)
                    for m in range(2):
                        if m:
                            dve.wait_ge(w_used[1], pair + 1)
                        else:
                            dve.wait_ge(bank_full[2], i + FULL0[f"ffn{layer}"][2] + 1)
                        mul(act_raw[:, m, :], bank[2 + m][:, :], rs).then_inc(bank_free[2 + m], 1)
                        dve.wait_ge(bank_free[2 + m], i + FREE0[f"ffn{layer}"][2 + m] + 1)
                        dve.wait_ge(gate_ready, i * 2 + (gates0 + m + 1))
                        mul(act_raw[:, m, :], act_raw[:, m, :], sig[:, m, :]).then_inc(h_raw_ready, 1)
                        dve.wait_ge(h_hi_ready, i * 2 + (FT * layer + m + 1))
                        dve.tensor_tensor(tile(h_lo, i * 2 + m), act_raw[:, m, :],
                                          tile(h_hi, i * 2 + m).bitcast(F32), ALU.subtract).then_inc(h_split, 1)
                    split_weights(1, pair + 1)
                    dve.wait_ge(h_split, i * 2 + (FT * layer + 2))
                clear_sum()
                if layer == 0:
                    with dve.Fori(0, KT // 2) as i:
                        body(i, False)
                else:
                    with dve.Fori(0, KT // 2 - 1) as i:
                        body(i, False)
                    body(KT // 2 - 1, True)

            ffn(0, 1, V_RET)
            inverse_rms(1)
            inverse_columns(6, "norm1", 1)

            dve.wait_ge(rope_loaded, 16)
            mul(rope[:, :, :], rope[:, :, :], repeated(rs, 1, 2)).then_inc(rope_scaled, 1)
            dve.wait_ge(rope_scaled, 1)
            with dve.Fori(0, H) as h:
                pair = h * 3 + PAIR0["ret"]
                free = [h * 3 + FREE0["ret"][b] for b in range(8)]
                t_bufs = [gate[:, n, :] for n in range(4)]

                def full(b, per_head, nth):
                    dve.wait_ge(bank_full[b], h * per_head + (FULL0["ret"][b] + nth))

                def rotate(which):
                    lo, hi = bank[2 * which], bank[2 * which + 1]
                    full(2 * which, 3, 1)
                    dve.wait_ge(w_used[which], pair + 1)
                    mul(t_bufs[0], lo[:, :], rope[:, 0, :])
                    mul(t_bufs[1], lo[:, :], rope[:, 1, :]).then_inc(bank_free[2 * which], 1)
                    mul(t_bufs[2], hi[:, :], rope[:, 1, :])
                    mul(t_bufs[3], hi[:, :], rope[:, 0, :]).then_inc(bank_free[2 * which + 1], 1)
                    dve.wait_ge(bank_free[2 * which + 1], free[2 * which + 1] + 1)
                    dve.tensor_tensor(qk[:, 2 * which, :], t_bufs[0], t_bufs[2], ALU.subtract)
                    dve.tensor_tensor(qk[:, 2 * which + 1, :], t_bufs[1], t_bufs[3], ALU.add).then_inc(rope_ready, 1)
                    dve.wait_ge(rope_ready, h * 2 + (which + 1))

                def scale_gate(m):
                    if m % 2:
                        dve.wait_ge(w_used[m // 2], pair + 3)
                    else:
                        full(4 + m, 3, 2)
                    mul(gate[:, m, :], bank[4 + m][:, :], rs).then_inc(bank_free[4 + m], 1)

                for which in range(2):
                    split_weights(which, pair + 1)
                    rotate(which)
                for s in range(2):
                    split_weights(s, pair + 2)
                dve.wait_ge(decay_loaded, h * 16 + 16)
                for jt in range(TT):
                    full(jt, 2 if jt % 2 else 3, 1 if jt % 2 else 2)
                    w = SEQ - P * jt
                    mul(scores[jt], bank[jt][:, 0:w], decay[:, 0:w]).then_inc(bank_free[jt], 1)
                scale_gate(0)
                for it in range(TT):
                    full(it, 2 if it % 2 else 3, 2 if it % 2 else 3)
                    dve.bn_stats(stats[:, it, :], bank[it][:, :]).then_inc(ret_step, 1)
                dve.wait_ge(ret_step, h * 5 + 4)
                scale_gate(1)
                for it in range(TT):
                    last = dve.bn_aggr(moments[:, it, :], stats[:, it, :])
                last.then_inc(var_ready, 1)
                dve.wait_ge(std_ready, h + 1)
                dve.reciprocal(o_rstd[:, :], o_std[:, :]).then_inc(ret_step, 1)
                dve.wait_ge(ret_step, h * 5 + 5)
                for it in range(TT):
                    dve.tensor_scalar(o_norm[:, it, :], bank[it][:, :], moments[:, it, 0:1], o_rstd[:, it:it + 1],
                                      ALU.subtract, ALU.mult).then_inc(bank_free[it], 1)
                split_weights(0, pair + 3)
                for m in range(2, 4):
                    scale_gate(m)
                split_weights(1, pair + 3)

                def low(m):
                    dve.wait_ge(ret_hi_ready, h * 4 + (m + 1))
                    dve.tensor_tensor(tile(y_lo, h * 4 + m), act_raw[:, m % 2, :], tile(y_hi, h * 4 + m).bitcast(F32),
                                      ALU.subtract).then_inc(ret_split, 1)

                for m in range(4):
                    full(4 + m, [3, 2, 3, 1][m], [3, 2, 3, 1][m])
                    dve.wait_ge(gate_ready, h * 4 + (FT + m + 1))
                    if m >= 2:
                        dve.wait_ge(ret_split, h * 4 + (m - 1))
                    dve.scalar_tensor_tensor(out=act_raw[:, m % 2, :], in0=bank[4 + m][:, :],
                                             scalar=vecs[:, bass.ds(h * 4 + (V_GN + m), 1)], in1=gate[:, m, :],
                                             op0=ALU.mult, op1=ALU.mult).then_inc(bank_free[4 + m], 1)
                    if m:
                        low(m - 1)
                low(3)
                dve.wait_ge(ret_split, h * 4 + 4)
            clear_sum()
            with dve.Fori(0, KT // 2) as i:
                for s in range(2):
                    dve.wait_ge(w_used[s], i + PAIR0["wo"] + 1)
                    add_to_x(i * 2 + s, bank[s][:, :]).then_inc(bank_free[s], 1)
                    dve.wait_ge(bank_free[s], i + (FREE0["wo"][s] + 1))
                    gained(2, i * 2 + s, s, V_FFN1)
                    add_square(2, i * 2 + s)
                    u_low(2, i * 2 + s, s)
                    split_weights(s, i + PAIR0["wo"] + 1)
                dve.wait_ge(u_split, i * 2 + (KT * 2 + 2))
            inverse_rms(2)
            ffn(1, 3, V_FINAL)
            inverse_columns(7, "norm3", 2)
            for t in range(TT):
                dve.wait_ge(bank_full[2 * t + 1], FULL0["store"][2 * t + 1] + 1)
                dve.tensor_scalar(out_sb[:, t, 512:1024], bank[2 * t + 1][:, :], rs_col[:, t:t + 1], None,
                                  ALU.mult).then_inc(out_right, 1)

        @block.gpsimd
        def _(pool):
            steps = [0]

            def step(ins):
                steps[0] += 1
                ins.then_inc(pool_step, 1)

            def settle():
                pool.wait_ge(pool_step, steps[0])

            def mul(o, a, b):
                return pool.tensor_tensor(o, a, b, ALU.mult)

            pool.memset(fb[:, :, :, :], 0.0).then_inc(fb_zeroed, 1)
            pool.wait_ge(ident_loaded, 16)
            step(pool.tensor_tensor(d_mask, ident[0:2 * N, 0:N], ident[0:2 * N, N:2 * N], ALU.add))
            pool.wait_ge(d_loaded, 64)
            d_flat = d_diag[:, :, :].rearrange("p j n -> p (j n)")
            step(mul(d_flat, d_flat, d_gain))
            settle()
            step(mul(d_diag[:, :, :], d_diag[:, :, :], repeated(d_mask, 1, J)))
            settle()
            pool.wait_ge(bt_ready, 2)
            b, fill = S5_AT[("lam", 0)]
            pool.wait_ge(bank_free[b], fill + 1)
            pool.wait_ge(fb_zeroed, 1)
            t = [pool_tmp[:, i, :, :, :].rearrange("p j k n -> p (j k n)").rearrange("p (j n) -> p j n", j=J)
                 for i in range(2)]
            f = [repeated(lam_t[:, 2 + i, :], 2, N) for i in range(2)]
            for ri in range(2):
                step(mul(t[0], bt[:, ri, :, :], f[0]))
                step(mul(t[1], bt[:, 1 - ri, :, :], f[1]))
                settle()
                for half in range(2):
                    ps = slice(64 * half, 64 * half + 64)
                    pool.tensor_tensor(fb[ps, ri, :, N * half:N * half + N], t[0][ps], t[1][ps],
                                       ALU.add if ri else ALU.subtract).then_inc(fb_ready, 1)
                pool.wait_ge(fb_ready, 2 * ri + 2)
            for ri in range(2):
                b, fill = S5_AT[("ct", ri)]
                pool.wait_ge(bank_free[b], fill + 1)
            pool.memset(states[:, 0, :, :], 0.0).then_inc(state0_ready, 1)
            pool.wait_ge(powers_ready, 1)

            def add_diagonal(part):
                b, fill = S5_AT[("strip", NBLK // 2 * (part + 1) - 1)]
                pool.wait_ge(bank_free[b], fill + 1)
                js = slice(J // 2 * part, J // 2 * part + J // 2)
                pool.tensor_tensor(strip[:, js, 0:N], strip[:, js, 0:N], d_diag[:, js, :], ALU.add).then_inc(diag_ready, 1)

            for k in range(NBLK):
                js = slice(JB * k, JB * k + JB)
                t = [pool_tmp[:, i, :, :, :] for i in range(2)]
                c = [repeated(ct[:, i, js, :], 2, STEPS) for i in range(2)]
                w = [repeated(powers[:, i, 0:STEPS, js].rearrange("p k j -> p j k"), 3, N) for i in range(2)]
                step(mul(t[0], c[0], w[0]))
                step(mul(t[1], c[1], w[1]))
                settle()
                step(pool.tensor_tensor(r_tc[:, 0, js, :, :], t[0], t[1], ALU.add))
                settle()
                step(mul(t[0], c[1], w[0]))
                step(mul(t[1], c[0], w[1]))
                settle()
                pool.tensor_tensor(r_tc[:, 1, js, :, :], t[0], t[1], ALU.subtract).then_inc(tc_ready, 1)
                pool.wait_ge(tc_ready, k + 1)
            for part in range(2):
                add_diagonal(part)


_INS = ["x", "s5_norm", "s5_lambda_re", "s5_lambda_im", "s5_log_step", "s5_b_re", "s5_b_im", "s5_c_re", "s5_c_im",
        "s5_d", "s5_glu_w", "s5_glu_b", "ret_norm", "ret_w_qkvg", "ret_gn_w", "ret_w_o", "ffn_norm", "ffn_w_gate",
        "ffn_w_up", "ffn_w_down", "final_norm"]


def _constants():
    f = np.float32
    inv_freq = (f(1.0) / (f(10000.0) ** np.linspace(0.0, 1.0, HD // 2, dtype=f))).astype(f)
    angle = (np.arange(SEQ, dtype=f)[:, None] * inv_freq[None, :]).astype(f).astype(np.float64)
    rope = np.concatenate([np.cos(angle).T, np.sin(angle).T], axis=1).astype(f)
    log_gamma = np.log1p(-np.exp2(-5.0 - np.arange(H)))
    key, query = np.arange(P)[:, None], np.arange(SEQ)[None, :]
    decay = np.exp(log_gamma[:, None, None] * np.abs(query - key)) * HD ** -0.5
    decay = np.where(query // CHUNK >= key // CHUNK, decay, 0.0)
    decay = np.ascontiguousarray(decay.transpose(1, 0, 2)).reshape(P, H * SEQ).astype(f)
    return {"const_ident": np.eye(P, dtype=f), "const_rope": rope, "const_decay": decay}


def kernel(**inputs):
    import concourse.bacc as _bacc
    from concourse.bass_utils import run_bass_kernel_spmd as _run

    nc = _bacc.Bacc("TRN2", target_bir_lowering=False, num_devices=1)
    arrays, args = {}, []
    for name in _INS:
        arrays[f"in_{name}_dram"] = np.ascontiguousarray(inputs[name])
    for name, a in _constants().items():
        arrays[f"in_{name}_dram"] = a
    for name, a in arrays.items():
        args.append(nc.dram_tensor(name, a.shape, mybir.dt.from_np(a.dtype), kind="ExternalInput").ap())
    args.append(nc.dram_tensor("out_0_dram", (1, SEQ, D), F32, kind="ExternalOutput").ap())
    trunk(nc, *args)
    r = _run(nc, [arrays], core_ids=[0])
    return r.results[0]["out_0_dram"]
```
